# Optimizing a Trainium2 kernel written in Bass

```python
import math
import numpy as np
import jax
import jax.numpy as jnp
from jax import lax

D_MODEL = 1024
BATCH = 1
SEQ = 512
DEPTH = 1
DEC_BATCH = 8
DEC_SEQ = 1
PAST_LEN = 2048
PAGE_SIZE = 128

HEAD_DIM = 64
N_HEADS = D_MODEL // HEAD_DIM
N_KV = 4
HPG = N_HEADS // N_KV
CMP_STRIDE = 16
CMP_BLOCK = 2 * CMP_STRIDE
CMP_HIDDEN = HEAD_DIM
SEL_BLOCK = 64
N_SELECT = 16
WINDOW = 512
Q_BLOCK = 128
S5_WIDTH = D_MODEL // 2
S5_CH = 16
S5_GROUPS = S5_WIDTH // S5_CH
S5_STATE = 64
D_FF = 4 * D_MODEL
D_Q = N_HEADS * HEAD_DIM
D_KV = N_KV * HEAD_DIM
D_IN = D_Q + 6 * D_KV + 3 * N_HEADS + S5_WIDTH + 2 * D_MODEL
SPLITS = [D_Q, D_Q + 6 * D_KV, D_Q + 6 * D_KV + 3 * N_HEADS, D_Q + 6 * D_KV + 3 * N_HEADS + S5_WIDTH]
EPS = 1e-6
NEG = -1e30
FORCE = 1e4

WIN_CACHE = min(WINDOW, PAST_LEN)
N_PAGES = PAST_LEN // PAGE_SIZE
N_PHYS = DEC_BATCH * N_PAGES + max(1, (DEC_BATCH * N_PAGES) // 4)

kernel_name = 'nsa_s5_gated_hybrid_step'

def rmsnorm(x, g):
    x32 = x.astype(jnp.float32)
    y = x32 * lax.rsqrt(jnp.mean(x32 * x32, axis=-1, keepdims=True) + EPS)
    return (y * g.astype(jnp.float32)).astype(x.dtype)

def masked_softmax(s, mask):
    s = jnp.where(mask, s.astype(jnp.float32), NEG)
    return jnp.where(mask, jax.nn.softmax(s, axis=-1), 0.0)

def split_proj(h, w_in):
    b, t = h.shape[0], h.shape[1]
    z = jnp.einsum('btd,de->bte', h, w_in)
    q, kv, gn, u, gm = jnp.split(z, SPLITS, axis=-1)
    q = q.reshape(b, t, N_KV, HPG, HEAD_DIM)
    kv = kv.reshape(b, t, 3, 2, N_KV, HEAD_DIM)
    gn = gn.reshape(b, t, N_KV, HPG, 3)
    return q, kv, gn, u, gm

def compress(k, pe, w1, w2):
    b, t = k.shape[0], k.shape[1]
    nch = t // CMP_STRIDE
    ch = k[:, : nch * CMP_STRIDE].reshape(b, nch, CMP_STRIDE, N_KV, HEAD_DIM)
    first = jnp.einsum('bnsgd,sdh->bngh', ch, w1[:CMP_STRIDE])
    second = jnp.einsum('bnsgd,sdh->bngh', ch, w1[CMP_STRIDE:])
    pos = jnp.einsum('sd,sdh->h', pe, w1)
    pre = first[:, :-1] + second[:, 1:] + pos
    return jnp.einsum('bngh,hd->bngd', jax.nn.gelu(pre), w2)

def sel_blocks(kv):
    b, t = kv.shape[0], kv.shape[1]
    nsel = -(-t // SEL_BLOCK)
    kv = jnp.pad(kv, ((0, 0), (0, nsel * SEL_BLOCK - t), (0, 0), (0, 0), (0, 0)))
    kv = kv.reshape(b, nsel, SEL_BLOCK, 2, N_KV, HEAD_DIM)
    return (jnp.transpose(kv[:, :, :, 0], (0, 3, 1, 2, 4)),
            jnp.transpose(kv[:, :, :, 1], (0, 3, 1, 2, 4)))

def nsa_attend(q, gates, qpos, kc, vc, ks, vs, kw, vw, kw_pos):
    scale = HEAD_DIM ** -0.5
    nc = kc.shape[1]
    c_end = jnp.arange(nc) * CMP_STRIDE + CMP_BLOCK - 1
    s = jnp.einsum('bqghd,bngd->bqghn', q, kc) * scale
    p = masked_softmax(s, (c_end[None, :] <= qpos[:, None])[None, :, None, None, :])
    o_cmp = jnp.einsum('bqghn,bngd->bqghd', p.astype(vc.dtype), vc)
    imp = p.sum(axis=3)
    nsel = ks.shape[2]
    j = np.arange(nsel)
    lo = np.clip((j * SEL_BLOCK - CMP_BLOCK) // CMP_STRIDE + 1, 0, nc)
    hi = np.clip((j * SEL_BLOCK + SEL_BLOCK - 1) // CMP_STRIDE + 1, 0, nc)
    cs = jnp.concatenate([jnp.zeros_like(imp[..., :1]), jnp.cumsum(imp, axis=-1)], axis=-1)
    imp_sel = cs[..., hi] - cs[..., lo]
    jj = jnp.arange(nsel)
    cur = qpos // SEL_BLOCK
    forced = (jj[None, :] == 0) | (jj[None, :] == cur[:, None]) | (jj[None, :] == cur[:, None] - 1)
    valid = jj[None, :] * SEL_BLOCK <= qpos[:, None]
    score = jnp.where(valid[None, :, None, :],
                      jnp.where(forced[None, :, None, :], FORCE, imp_sel), -1.0)
    k_sel = min(N_SELECT, nsel)
    _, idx = lax.top_k(score, k_sel)
    bi = jnp.arange(q.shape[0])[:, None, None, None]
    gi = jnp.arange(N_KV)[None, None, :, None]
    k_g = ks[bi, gi, idx]
    v_g = vs[bi, gi, idx]
    s = jnp.einsum('bqghd,bqgksd->bqghks', q, k_g) * scale
    tok = idx[..., None] * SEL_BLOCK + jnp.arange(SEL_BLOCK)
    mask = (tok <= qpos[None, :, None, None, None])[:, :, :, None]
    shp = s.shape
    p = masked_softmax(s.reshape(shp[:4] + (-1,)), mask.reshape(mask.shape[:4] + (-1,)))
    o_slc = jnp.einsum('bqghks,bqgksd->bqghd', p.reshape(shp).astype(v_g.dtype), v_g)
    s = jnp.einsum('bqghd,bwgd->bqghw', q, kw) * scale
    rel = qpos[:, None] - kw_pos[None, :]
    wmask = (rel >= 0) & (rel < WINDOW) & (kw_pos[None, :] >= 0)
    p = masked_softmax(s, wmask[None, :, None, None, :])
    o_win = jnp.einsum('bqghw,bwgd->bqghd', p.astype(vw.dtype), vw)
    g = jax.nn.sigmoid(gates)
    return g[..., 0:1] * o_cmp + g[..., 1:2] * o_slc + g[..., 2:3] * o_win

def s5(u, h0, w):
    b, t = u.shape[0], u.shape[1]
    f32 = jnp.float32
    uc = u.astype(f32).reshape(b, t, S5_GROUPS, S5_CH)
    lam = lax.complex(w['s5_a_re'].astype(f32), w['s5_a_im'].astype(f32))
    dt = jnp.exp(w['s5_log_dt'].astype(f32))[:, None]
    a_bar = jnp.exp(lam * dt)
    b_c = lax.complex(w['s5_b_re'].astype(f32), w['s5_b_im'].astype(f32))
    b_bar = ((a_bar - 1.0) / lam)[..., None] * b_c
    c_c = lax.complex(w['s5_c_re'].astype(f32), w['s5_c_im'].astype(f32))
    bu = jnp.einsum('gnc,btgc->btgn', b_bar, uc.astype(jnp.complex64))
    a = jnp.broadcast_to(a_bar, bu.shape)

    def combine(e1, e2):
        a1, b1 = e1
        a2, b2 = e2
        return a1 * a2, a2 * b1 + b2

    a_cum, b_cum = lax.associative_scan(combine, (a, bu), axis=1)
    h = b_cum + a_cum * h0[:, None]
    y = jnp.einsum('gcn,btgn->btgc', c_c, h).real + w['s5_d'].astype(f32).reshape(S5_GROUPS, S5_CH) * uc
    return y.reshape(b, t, S5_WIDTH).astype(u.dtype), h[:, -1]

def merge_and_mlp(x, o_nsa, y_s5, gm, w):
    b, t = x.shape[0], x.shape[1]
    z = jax.nn.gelu(y_s5)
    o_s5 = z * jax.nn.sigmoid(z @ w['s5_w_glu'] + w['s5_b_glu'])
    g_a, g_b = jnp.split(gm, 2, axis=-1)
    merged = (jax.nn.sigmoid(g_a) * (o_nsa.reshape(b, t, D_Q) @ w['w_branch_nsa'])
              + jax.nn.sigmoid(g_b) * (o_s5 @ w['w_branch_s5']))
    x = x + rmsnorm(merged @ w['w_out'], w['norm_mix_post'])
    hm = rmsnorm(x, w['norm_mlp_pre'])
    f = jnp.square(jax.nn.relu(hm @ w['w_mlp_up'])) @ w['w_mlp_down']
    return x + rmsnorm(f, w['norm_mlp_post'])

def stack_state(h, dtype):
    return jnp.stack([h.real, h.imag], axis=-1).astype(dtype)

def prompt_layer(x, w):
    b, t = x.shape[0], x.shape[1]
    h = rmsnorm(x, w['norm_mix_pre'])
    q, kv, gn, u, gm = split_proj(h, w['w_in'])
    kc = compress(kv[:, :, 0, 0], w['cmp_pe_k'], w['cmp_w1_k'], w['cmp_w2_k'])
    vc = compress(kv[:, :, 0, 1], w['cmp_pe_v'], w['cmp_w1_v'], w['cmp_w2_v'])
    ks, vs = sel_blocks(kv[:, :, 1])
    kw_pad = jnp.pad(kv[:, :, 2], ((0, 0), (WINDOW, 0), (0, 0), (0, 0), (0, 0)))
    nqb = t // Q_BLOCK
    q_b = q.reshape(b, nqb, Q_BLOCK, N_KV, HPG, HEAD_DIM).swapaxes(0, 1)
    g_b = gn.reshape(b, nqb, Q_BLOCK, N_KV, HPG, 3).swapaxes(0, 1)
    starts = jnp.arange(nqb, dtype=jnp.int32) * Q_BLOCK

    def block(args):
        qb, gb, s0 = args
        qpos = s0 + jnp.arange(Q_BLOCK, dtype=jnp.int32)
        kvw = lax.dynamic_slice_in_dim(kw_pad, s0, WINDOW + Q_BLOCK, axis=1)
        kw_pos = s0 - WINDOW + jnp.arange(WINDOW + Q_BLOCK, dtype=jnp.int32)
        return nsa_attend(qb, gb, qpos, kc, vc, ks, vs, kvw[:, :, 0], kvw[:, :, 1], kw_pos)

    o = lax.map(block, (q_b, g_b, starts))
    o = o.swapaxes(0, 1).reshape(b, t, N_KV, HPG, HEAD_DIM)
    y_s5, h_last = s5(u, jnp.zeros((b, S5_GROUPS, S5_STATE), jnp.complex64), w)
    y = merge_and_mlp(x, o, y_s5, gm, w)
    return y, kv[:, :, 0], kv[:, :, 1], kw_pad[:, -WIN_CACHE:], stack_state(h_last, x.dtype)

def gather_pages(cache, page_table):
    g = cache[page_table]
    return g.reshape(page_table.shape[0], page_table.shape[1] * PAGE_SIZE, 2, N_KV, HEAD_DIM)

def sample_layer(x, cache_kv_cmp, cache_kv_slc, state_kv_win, state_s5, page_table, w):
    t = x.shape[1]
    past = page_table.shape[1] * PAGE_SIZE
    h = rmsnorm(x, w['norm_mix_pre'])
    q, kv, gn, u, gm = split_proj(h, w['w_in'])
    kv_cmp = jnp.concatenate([gather_pages(cache_kv_cmp, page_table), kv[:, :, 0].astype(cache_kv_cmp.dtype)], axis=1)
    kc = compress(kv_cmp[:, :, 0], w['cmp_pe_k'], w['cmp_w1_k'], w['cmp_w2_k'])
    vc = compress(kv_cmp[:, :, 1], w['cmp_pe_v'], w['cmp_w1_v'], w['cmp_w2_v'])
    kv_slc = jnp.concatenate([gather_pages(cache_kv_slc, page_table), kv[:, :, 1].astype(cache_kv_slc.dtype)], axis=1)
    ks, vs = sel_blocks(kv_slc)
    kvw = jnp.concatenate([state_kv_win, kv[:, :, 2].astype(state_kv_win.dtype)], axis=1)
    win_rows = state_kv_win.shape[1]
    kw_pos = past - win_rows + jnp.arange(win_rows + t, dtype=jnp.int32)
    qpos = past + jnp.arange(t, dtype=jnp.int32)
    o = nsa_attend(q, gn, qpos, kc, vc, ks, vs, kvw[:, :, 0], kvw[:, :, 1], kw_pos)
    st = state_s5.astype(jnp.float32)
    y_s5, h_last = s5(u, lax.complex(st[..., 0], st[..., 1]), w)
    y = merge_and_mlp(x, o, y_s5, gm, w)
    return y, kv[:, :, 0], kv[:, :, 1], kvw[:, -win_rows:], stack_state(h_last, state_s5.dtype)

def setup_inputs(seed: int = 0) -> dict:
    key = jax.random.key(seed)
    ks = jax.random.split(key, 40)
    nrm = jax.random.normal
    f32 = jnp.float32
    page_table = jax.random.permutation(ks[6], N_PHYS)[: DEC_BATCH * N_PAGES].reshape(DEC_BATCH, N_PAGES).astype(jnp.int32)
    a_im = math.pi * jnp.arange(S5_STATE, dtype=f32)[None, :] + 0.01 * nrm(ks[19], (S5_GROUPS, S5_STATE), f32)
    return {
        'x_prompt': nrm(ks[0], (BATCH, SEQ, D_MODEL), f32),
        'x_sample': nrm(ks[1], (DEC_BATCH, DEC_SEQ, D_MODEL), f32),
        'cache_kv_cmp': nrm(ks[2], (N_PHYS, PAGE_SIZE, 2, N_KV, HEAD_DIM), f32),
        'cache_kv_slc': nrm(ks[3], (N_PHYS, PAGE_SIZE, 2, N_KV, HEAD_DIM), f32),
        'state_kv_win': nrm(ks[4], (DEC_BATCH, WIN_CACHE, 2, N_KV, HEAD_DIM), f32),
        'state_s5': 0.1 * nrm(ks[5], (DEC_BATCH, S5_GROUPS, S5_STATE, 2), f32),
        'page_table': page_table,
        'norm_mix_pre': 1.0 + 0.05 * nrm(ks[7], (D_MODEL,), f32),
        'norm_mix_post': 1.0 + 0.05 * nrm(ks[8], (D_MODEL,), f32),
        'norm_mlp_pre': 1.0 + 0.05 * nrm(ks[9], (D_MODEL,), f32),
        'norm_mlp_post': 1.0 + 0.05 * nrm(ks[10], (D_MODEL,), f32),
        'w_in': nrm(ks[11], (D_MODEL, D_IN), f32) * D_MODEL ** -0.5,
        'cmp_pe_k': 0.1 * nrm(ks[12], (CMP_BLOCK, HEAD_DIM), f32),
        'cmp_w1_k': nrm(ks[13], (CMP_BLOCK, HEAD_DIM, CMP_HIDDEN), f32) * (CMP_BLOCK * HEAD_DIM) ** -0.5,
        'cmp_w2_k': nrm(ks[14], (CMP_HIDDEN, HEAD_DIM), f32) * CMP_HIDDEN ** -0.5,
        'cmp_pe_v': 0.1 * nrm(ks[15], (CMP_BLOCK, HEAD_DIM), f32),
        'cmp_w1_v': nrm(ks[16], (CMP_BLOCK, HEAD_DIM, CMP_HIDDEN), f32) * (CMP_BLOCK * HEAD_DIM) ** -0.5,
        'cmp_w2_v': nrm(ks[17], (CMP_HIDDEN, HEAD_DIM), f32) * CMP_HIDDEN ** -0.5,
        's5_a_re': -0.5 + 0.01 * nrm(ks[18], (S5_GROUPS, S5_STATE), f32),
        's5_a_im': a_im,
        's5_log_dt': jax.random.uniform(ks[20], (S5_GROUPS,), f32, math.log(0.001), math.log(0.1)),
        's5_b_re': nrm(ks[21], (S5_GROUPS, S5_STATE, S5_CH), f32) * (2 * S5_CH) ** -0.5,
        's5_b_im': nrm(ks[22], (S5_GROUPS, S5_STATE, S5_CH), f32) * (2 * S5_CH) ** -0.5,
        's5_c_re': nrm(ks[23], (S5_GROUPS, S5_CH, S5_STATE), f32) * S5_STATE ** -0.5,
        's5_c_im': nrm(ks[24], (S5_GROUPS, S5_CH, S5_STATE), f32) * S5_STATE ** -0.5,
        's5_d': nrm(ks[25], (S5_WIDTH,), f32),
        's5_w_glu': nrm(ks[26], (S5_WIDTH, S5_WIDTH), f32) * S5_WIDTH ** -0.5,
        's5_b_glu': 0.01 * nrm(ks[27], (S5_WIDTH,), f32),
        'w_branch_nsa': nrm(ks[28], (D_Q, D_MODEL), f32) * D_Q ** -0.5,
        'w_branch_s5': nrm(ks[29], (S5_WIDTH, D_MODEL), f32) * S5_WIDTH ** -0.5,
        'w_out': nrm(ks[30], (D_MODEL, D_MODEL), f32) * D_MODEL ** -0.5,
        'w_mlp_up': nrm(ks[31], (D_MODEL, D_FF), f32) * D_MODEL ** -0.5,
        'w_mlp_down': nrm(ks[32], (D_FF, D_MODEL), f32) * D_FF ** -0.5,
    }

def reference(x_prompt, x_sample, cache_kv_cmp, cache_kv_slc, state_kv_win, state_s5, page_table,
              norm_mix_pre, norm_mix_post, norm_mlp_pre, norm_mlp_post, w_in,
              cmp_pe_k, cmp_w1_k, cmp_w2_k, cmp_pe_v, cmp_w1_v, cmp_w2_v,
              s5_a_re, s5_a_im, s5_log_dt, s5_b_re, s5_b_im, s5_c_re, s5_c_im, s5_d, s5_w_glu, s5_b_glu,
              w_branch_nsa, w_branch_s5, w_out, w_mlp_up, w_mlp_down):
    w = {
        'norm_mix_pre': norm_mix_pre, 'norm_mix_post': norm_mix_post,
        'norm_mlp_pre': norm_mlp_pre, 'norm_mlp_post': norm_mlp_post, 'w_in': w_in,
        'cmp_pe_k': cmp_pe_k, 'cmp_w1_k': cmp_w1_k, 'cmp_w2_k': cmp_w2_k,
        'cmp_pe_v': cmp_pe_v, 'cmp_w1_v': cmp_w1_v, 'cmp_w2_v': cmp_w2_v,
        's5_a_re': s5_a_re, 's5_a_im': s5_a_im, 's5_log_dt': s5_log_dt,
        's5_b_re': s5_b_re, 's5_b_im': s5_b_im, 's5_c_re': s5_c_re, 's5_c_im': s5_c_im,
        's5_d': s5_d, 's5_w_glu': s5_w_glu, 's5_b_glu': s5_b_glu,
        'w_branch_nsa': w_branch_nsa, 'w_branch_s5': w_branch_s5, 'w_out': w_out,
        'w_mlp_up': w_mlp_up, 'w_mlp_down': w_mlp_down,
    }
    y_p = x_prompt
    y_s = x_sample
    for _ in range(DEPTH):
        y_p, kvc_p, kvs_p, win_p, s5_p = prompt_layer(y_p, w)
        y_s, kvc_s, kvs_s, win_s, s5_s = sample_layer(y_s, cache_kv_cmp, cache_kv_slc, state_kv_win, state_s5, page_table, w)
    return (y_p, y_s, kvc_p, kvs_p, win_p, s5_p, kvc_s, kvs_s, win_s, s5_s)


_drawn_inputs = setup_inputs


def setup_inputs(seed=0):
    import zlib

    import numpy as np

    out = dict(_drawn_inputs(seed))
    spreads = {}
    factors = {'cmp_pe_k': 5.095, 's5_a_re': 4.295, 's5_b_glu': 8.0}
    for name, (base, spread) in spreads.items():
        noise = np.random.default_rng([zlib.crc32(name.encode()), seed]).standard_normal(out[name].shape)
        drawn = base * np.exp(spread * noise) if base else spread * noise
        out[name] = jnp.asarray(drawn.astype(out[name].dtype))
    for name, factor in factors.items():
        out[name] = (out[name] * factor).astype(out[name].dtype)
    return out
```

```python
from contextlib import ExitStack

import numpy as np
import concourse.bass as bass
from concourse import mybir

ALU = mybir.AluOpType
ACT = mybir.ActivationFunctionType
AX = mybir.AxisListType.X
F32 = mybir.dt.float32
BF16 = mybir.dt.bfloat16
I32 = mybir.dt.int32

P = 128
D = 1024
KD = D // P
T = 512
TT = T // P
NB = 8
NT = T + NB
HALF = NT // 2
PAGE = 128
N_PAGES = 16
N_PHYS = 160
NG, HPG, DH = 4, 4, 64
NH = NG * HPG
KVW = 2 * NG * DH
STRIDE = 16
NCH = N_PAGES * PAGE // STRIDE
NC = NCH - 1
NCP = T // STRIDE - 1
SELB = 64
NSEL = 33
TOPK = 16
WIN = 512
G5, N5, C5 = 32, 64, 16
NST = G5 // 2
FF = 4096
KF = FF // P
EPS = 1e-6
NEG = -1e30
FORCE = 1e4
C_KV = 1024
C_GN = C_KV + 3 * KVW
C_U = C_GN + 3 * NH
C_GM = C_U + 512
TWO_PI = 2.0 * np.pi
RND = 12582912.0

SLOT = 4096
NS = 3

CO_ID = 0
CO_MASK = CO_ID + P
CO_CMASK = CO_MASK + P
CO_ROWV = CO_CMASK + TT * NCP
CO_HSUM = CO_ROWV + TT
CO_HSUMT = CO_HSUM + 32
CO_BM = CO_HSUMT + P
CO_BMT = CO_BM + NB
CO_HM = CO_BMT + P
CO_ROW = CO_HM + NH
CO_GM16 = CO_ROW + 2
CO_N = CO_GM16 + 4 * NB


def shape_constants():
    c = np.zeros((P, CO_N), np.float32)
    i = np.arange(P)
    c[:, CO_ID:CO_ID + P] = np.eye(P)
    c[:, CO_MASK:CO_MASK + P] = np.where(i[None, :] > i[:, None], NEG, 0)
    for t in range(TT):
        q = i + P * t
        ok = (16 * np.arange(NCP) + 31)[None, :] <= q[:, None]
        c[:, CO_CMASK + NCP * t:CO_CMASK + NCP * (t + 1)] = np.where(ok, 0, NEG)
        c[:, CO_ROWV + t] = q >= 31
    c[:, CO_HSUM:CO_HSUM + 32] = i[:, None] // HPG == np.arange(32)[None, :]
    c[:32, CO_HSUMT:CO_HSUMT + P] = i[None, :] // HPG == np.arange(32)[:, None]
    c[:, CO_BM:CO_BM + NB] = i[:, None] // NH == np.arange(NB)[None, :]
    c[:NB, CO_BMT:CO_BMT + P] = i[None, :] // NH == np.arange(NB)[:, None]
    c[:, CO_HM:CO_HM + NH] = i[:, None] % NH == np.arange(NH)[None, :]
    c[:, CO_ROW], c[:, CO_ROW + 1] = 2 * i, 2 * (i % 8)
    c[:, CO_GM16:CO_GM16 + 4 * NB] = (np.arange(4 * NB) % NG)[None, :] == (i // HPG)[:, None]
    j = np.arange(NSEL)
    tie = np.broadcast_to((j[None, :] < j[:, None]).astype(np.float32), (32, NSEL, NSEL)).copy()
    return c, tie


def stream_plan():
    plan = [("win", (C_U, 512), 1, 0)]
    plan += [("win", (C_KV + KVW * c, 512), 1, 0) for c in range(3)]
    plan += [("win", (C_GN, 3 * NH), 1, 0)]
    plan += [("q", (p,), 8, 0) for p in range(2)]
    for b in range(NB):
        plan += [("cmp", (b, half), 0, 1) for half in range(2)]
    plan += [("cmp", (NB, half), 1, 0) for half in range(2)]
    for q in range(4):
        plan += [("kpage", (q, bh), 8, 8) for bh in range(2)]
    plan += [("winrows", (0, bh), 4, 0) for bh in range(2)]
    plan += [("winrows", (1, bh), 4, 0) for bh in range(2)]
    plan += [("vpage", (b,), 8, 8) for b in range(NB)]
    plan += [("glu", (), 1, 0)]
    plan += [("mix", (m,), 7, 0) for m in range(KD)]
    plan += [("out", (m,), 1, 0) for m in range(2)]
    plan += [("up", (m,), 1, 0) for m in range(KF // 4)]
    plan += [("down", (m,), 1, 0) for m in range(KD)]
    return plan


PLAN = stream_plan()
SLAB = {(k, a): n for n, (k, a, _, _) in enumerate(PLAN)}


def landed_counts(who):
    counts, total = [], [0] * NS
    for n, entry in enumerate(PLAN):
        total[n % NS] += 16 * entry[2 + who]
        counts.append(total[n % NS])
    return counts


LANDED = [landed_counts(0), landed_counts(1)]


def projection_units():
    units = [("gemm", ("win", (C_U, 512)), m, P, ("u", m)) for m in range(4)]
    units += [("bb", ri, q) for ri in range(2) for q in range(4)]
    units += [("cc", ri, q) for ri in range(2) for q in range(4)]
    units += [("h0",), ("bus",)]
    rest = []
    prev = None
    for c in range(3):
        for m in range(4):
            rest.append(("gemm", ("win", (C_KV + KVW * c, 512)), m, P, ("kv", c, m)))
            if prev is not None:
                rest.append(("tr", *prev))
            prev = (c, m)
    rest.append(("tr", *prev))
    rest.append(("gemm", ("win", (C_GN, 3 * NH)), 0, 3 * NH, ("gn",)))
    rest.append(("gemm", ("q", (0,)), 0, P, ("q", 0)))
    rest.append(("trg",))
    rest += [("gemm", ("q", (i // 4,)), i % 4, P, ("q", i)) for i in range(1, 8)]
    return units, rest


HEAD_UNITS, REST_UNITS = projection_units()
N_UNITS_A = len(HEAD_UNITS) + len(REST_UNITS)
KV_TILES = [(c, m) for c in range(3) for m in range(4)]


def build(nc, a):
    with ExitStack() as ctx:
        def sb(name, shape, dt=F32):
            return ctx.enter_context(nc.sbuf_tensor(name, shape, dt))

        def sem(name):
            return ctx.enter_context(nc.semaphore(name))

        consts = sb("consts", [P, CO_N])
        idb = sb("idb", [P, P], BF16)
        maskb = sb("maskb", [P, P], BF16)
        pages = sb("pages", [P, NB * N_PAGES], I32)
        pages8 = sb("pages8", [P, NB], I32)
        row_kv = sb("row_kv", [P, 2, NB * N_PAGES], I32)
        row_cmp = sb("row_cmp", [P, 2, NB], I32)
        hT = sb("hT", [P, KD, NT])
        QO = sb("QO", [P, 2 * KD * NT])
        KVU = sb("KVU", [P, 12 * NT])
        kvs = sb("kvs", [NB, 3 * KVW])
        R = sb("R", [P, 16896])
        stream = sb("stream", [P, NS, SLOT])
        small = sb("small", [P, 1600])

        qT = QO[:, 0:KD * NT].rearrange("p (k t) -> p k t", t=NT)
        oT = QO[:, KD * NT:].rearrange("p (k t) -> p k t", t=NT)
        kT = KVU[:, 0:4 * NT].rearrange("p (k t) -> p k t", t=NT)
        vtm = KVU[:, 4 * NT:4 * NT + 2048].rearrange("p (t c) -> p t c", t=TT)
        uT = KVU[:, 8 * NT:12 * NT].rearrange("p (k t) -> p k t", t=NT)

        ident = consts[:, CO_ID:CO_ID + P]
        used = [0]

        def tiny(n):
            used[0] += n
            assert used[0] <= 1600
            return small[:, used[0] - n:used[0]]

        gT = tiny(2 * KD).rearrange("p (w k) -> p w k", w=2)
        are, aim, ldt = tiny(NST), tiny(NST), tiny(NST)
        dt, mag, ang, ang2, sn, sh, cs = (tiny(NST) for _ in range(7))
        abr, abi, nabi, den, cor, coi, s5t, s5u = (tiny(NST) for _ in range(8))
        ur, ui, tp0, tp1 = (tiny(NST) for _ in range(4))
        ssq, rstd = tiny(5), tiny(5)
        epsb = tiny(1)
        s5d, bglu = tiny(4), tiny(4)
        h0T = tiny(2 * NST * NB).rearrange("p (i r b) -> p i r b", i=NST, r=2)
        buS = tiny(2 * NST * NB).rearrange("p (i r b) -> p i r b", i=NST, r=2)
        hS = tiny(2 * NST * 9).rearrange("p (i r b) -> p i r b", i=NST, r=2)
        sst = tiny(4 * NB).rearrange("p (k b) -> p k b", k=4)
        gtm = tiny(TT * 3 * NH).rearrange("p (t c) -> p t c", t=TT)
        gs8 = tiny(3 * NH)
        gsTs = tiny(NB)
        pos = tiny(1)
        gd = tiny(3)
        dmx, dsm, dinv = tiny(3), tiny(3), tiny(3)
        amx, asm, ainv = tiny(4), tiny(4), tiny(4)
        cmx, csm = tiny(NH), tiny(NH)

        PS = ctx.enter_context(nc.psum_tensor("PS", [P, 8, 512], F32))

        consts_in = sem("consts_in")
        x_in = sem("x_in")
        pages_in = sem("pages_in")
        rows_ready = sem("rows_ready")
        perm_ready = sem("perm_ready")
        par_in = sem("par_in")
        slab_in = [sem(f"slab_in{i}") for i in range(NS)]
        rows_in = [sem(f"rows_in{i}") for i in range(NS)]
        slab_used = sem("slab_used")
        act_ch = sem("act_ch")
        dve_ch = sem("dve_ch")
        pool_ch = sem("pool_ch")
        masks_ready = sem("masks_ready")
        zero_ready = sem("zero_ready")
        root_ready = sem("root_ready")
        xn_ready = sem("xn_ready")
        xnt_full = sem("xnt_full")
        xnt_free = sem("xnt_free")
        pair_full = sem("pair_full")
        pair_free = sem("pair_free")
        ldt_ready = sem("ldt_ready")
        ang_ready = sem("ang_ready")
        trig_ready = sem("trig_ready")
        unit_ready = sem("unit_ready")
        bb_ready = sem("bb_ready")
        c_in = sem("c_in")
        h0_in = sem("h0_in")
        table_ready = sem("table_ready")
        bu_full = sem("bu_full")
        bu_free = sem("bu_free")
        h_ready = sem("h_ready")
        h_used = sem("h_used")
        y_full = sem("y_full")
        y_free = sem("y_free")
        st_full = sem("st_full")
        st_ready = sem("st_ready")
        kv_store = [sem(f"kv_store{i}") for i in range(4)]
        stores = sem("stores")
        copies = sem("copies")
        w1_in = sem("w1_in")
        pos_full = sem("pos_full")
        xt_full = sem("xt_full")
        xt_ready = sem("xt_ready")
        xt_used = sem("xt_used")
        acc_full = sem("acc_full")
        pre_ready = sem("pre_ready")
        gelu_ready = sem("gelu_ready")
        l2_full = sem("l2_full")
        l2_ready = sem("l2_ready")
        qpad_ready = sem("qpad_ready")
        sc_full = sem("sc_full")
        sc_max = sem("sc_max")
        sc_exp = sem("sc_exp")
        pc_ready = sem("pc_ready")
        imp_full = sem("imp_full")
        sel_ready = sem("sel_ready")
        selx_full = sem("selx_full")
        s_full = sem("s_full")
        smax = sem("smax")
        sexp = sem("sexp")
        p_ready = sem("p_ready")
        pt_full = sem("pt_full")
        pt_ready = sem("pt_ready")
        od_full = sem("od_full")
        cs_full = sem("cs_full")
        cs_max = sem("cs_max")
        cs_exp = sem("cs_exp")
        cs_done = sem("cs_done")
        as_full = sem("as_full")
        as_max = sem("as_max")
        as_exp = sem("as_exp")
        as_rec = sem("as_rec")
        as_p = sem("as_p")
        at_full = sem("at_full")
        at_a = sem("at_a")
        at_d = sem("at_d")
        ao_full = sem("ao_full")
        ao_free = sem("ao_free")
        z_ready = sem("z_ready")
        os5_ready = sem("os5_ready")
        mix_ready = sem("mix_ready")
        gain_in = sem("gain_in")
        x2_in = sem("x2_in")
        x1_ready = sem("x1_ready")
        f_ready = sem("f_ready")
        tie_in = sem("tie_in")
        od_ready = sem("od_ready")
        kz_ready = sem("kz_ready")
        ot_ready = sem("ot_ready")
        ot_full = sem("ot_full")
        s5_store = sem("s5_store")

        BBT = R[:, 0:4096].rearrange("p (r i c) -> p r i c", r=2, i=NST)
        CCT = R[:, 4096:8192].rearrange("p (r i c) -> p r i c", r=2, i=NST)
        BBP = R[:, 8192:12288].rearrange("p (r i c) -> p r i c", r=2, i=NST)
        CCP = R[:, 12288:16384].rearrange("p (r i c) -> p r i c", r=2, i=NST)
        TAB = R[:, 8192:16384].rearrange("p (s r i t) -> p s r i t", s=2, r=2, i=4)
        WK = R[:, 16384:16896]
        STO = R[0:9, 8192:12288].rearrange("p (i c r) -> p i c r", i=NST, r=2)
        bld = R[:, 0:512].rearrange("p (r i c) -> p r i c", r=2, i=NST)
        bwk = R[:, 512:1536].rearrange("p (r i c) -> p r i c", r=4, i=NST)
        xtm = KVU[:, 0:5 * D].rearrange("p (t d) -> p t d", d=D)
        xn = QO[:, 0:2 * D].rearrange("p (s d) -> p s d", s=2)
        junk = QO[:, 2 * D:3 * D]
        st0 = QO[0:NB, KD * NT:KD * NT + 4096].rearrange("b (i c r) -> b i r c", i=NST, r=2)
        W5 = [QO[:, KD * NT + NT * i:KD * NT + NT * (i + 1)] for i in range(8)]
        zst = QO[:, 2048:2048 + 2 * NT].rearrange("p (s t) -> p s t", s=2)
        kst = QO[:, 0:2048].rearrange("p (s t c) -> p s t c", s=4, t=TT)
        gsT = zst[0:3 * NH, 0, 0:T]

        XT = R[:, 0:1536].rearrange("p (s c) -> p s c", s=3)
        w1c = R[:, 1536:3584].rearrange("p (k s h) -> p k s h", k=2, s=8)
        SH = R[:, 3584:4096]
        PRE = R[:, 4096:4608]
        GEL = R[:, 4608:5120]
        w2 = R[:, 5120:5184]
        peT = R[:, 5184:5216].rearrange("p (k s) -> p k s", k=2)
        kcT = R[:, 5216:7520].rearrange("p (b q n) -> p b q n", b=9, q=2)
        vc = R[:, 7520:9824].rearrange("p (b c) -> p b c", b=9)
        ROWSP = R[:, 9824:9824 + 6144].rearrange("p (w g s d) -> p w g s d", w=3, g=4, s=8)
        QP = R[:, 9824:11872].rearrange("p (q b c) -> p q b c", q=2, b=NB)
        SA = R[:, 11872:13921]
        SW = R[:, 13921:14434]
        SC = R[:, 14434:14563]
        IMP = R[0:32, 14564:14697]
        SSEL = R[0:32, 14700:14733]
        SELX = R[:, 14740:14773]
        GH = R[:, 14780:14828]
        CMPA = R[0:32, 14828:15917].rearrange("p (j i) -> p j i", j=NSEL)
        CMPB = R[0:32, 1536:2625].rearrange("p (j i) -> p j i", j=NSEL)
        TIE = R[0:32, 2625:3714].rearrange("p (j i) -> p j i", j=NSEL)
        PTA = R[:, 1536:4096].rearrange("p (g c) -> p g c", c=P)
        PTN = R[0:NB, 4096:4352].rearrange("p (r c) -> p r c", r=2)
        PTC = R[:, 4352:4480]
        PNB = R[:, 4480:4496].rearrange("p (r b) -> p r b", r=2)
        OD = R[0:NH, 9824:11872].rearrange("p (x d) -> p x d", d=DH)
        OE = R[0:NH, 11872:13920].rearrange("p (x d) -> p x d", d=DH)
        OS = R[0:NH, 16160:16672].rearrange("p (b d) -> p b d", d=DH)
        KCZ = R[:, 16672:16796].rearrange("p (q j n) -> p q j n", q=2, j=2)
        KZ = R[:, 0:4096].rearrange("p (j k t) -> p j k t", j=2, k=4)
        PP = R[:, 9824:11872].rearrange("p (s r c) -> p s r c", s=2, r=2)
        PTP = R[:, 11872:13920].rearrange("p (s g c) -> p s g c", s=2, g=8)
        PTPC = R[:, 13920:14176].rearrange("p (s c) -> p s c", s=2)
        PCP = R[:, 14176:14176 + TT * NH * NCP].rearrange("p (t h n) -> p t h n", t=TT, h=NH)
        zT = R[:, 0:4 * NT].rearrange("p (k t) -> p k t", t=NT)
        sgl = R[:, 4 * NT:6 * NT].rearrange("p (s t) -> p s t", s=2)
        mxb = R[:, 6 * NT:14 * NT].rearrange("p (s k t) -> p s k t", s=2, k=4)
        mT = R[:, 14 * NT:22 * NT].rearrange("p (k t) -> p k t", t=NT)
        zo = R[:, 22 * NT:24 * NT].rearrange("p (s t) -> p s t", s=2)
        ytm = KVU[:, 0:5 * D].rearrange("p (t d) -> p t d", d=D)
        x1 = QO[:, 0:5 * D].rearrange("p (t d) -> p t d", d=D)
        xn2 = QO[:, 5 * D:7 * D].rearrange("p (s d) -> p s d", s=2)
        gain = QO[:, 7 * D:8 * D]
        fT = R[:, 0:KF * NT].rearrange("p (k t) -> p k t", t=NT)

        def slab(n):
            return stream[:, n % NS, :]

        def slab_page(kind, arg, x):
            if kind == "kpage":
                return (4 * arg[1] + x // 4) * N_PAGES + 4 * arg[0] + x % 4
            return arg[0] * N_PAGES + x

        def wait_slab(eng, n):
            if PLAN[n][2]:
                eng.wait_ge(slab_in[n % NS], LANDED[0][n])
            if PLAN[n][3]:
                eng.wait_ge(rows_in[n % NS], LANDED[1][n])

        def pair(u):
            return PS[:, 2 * (u % 2):2 * (u % 2) + 2, :]

        def halves(ap):
            return ap.rearrange("p (h t) -> p h t", h=2)

        UA = N_UNITS_A
        U_GLU = UA
        U_MIX = U_GLU + 4
        U_OUT = U_MIX + 4 * KD
        U_UP = U_OUT + 2 * KD
        U_DOWN = U_UP + KF
        RS = [(b, half, kind, s4) for b in range(NB + 1) for half in range(2) for kind in range(2) for s4 in range(4)]
        KR = [(q, b, p) for q in range(5) for b in range(NB) for p in range(2)]
        N_RS = len(RS)
        TASKS = [(t, p, h, j) for t in range(TT) for p in range(2) for h in range(HPG) for j in range(2)]
        NTK = len(TASKS)
        OUT_ORDER = [("g", 0)]
        for m_ in range(1, KD):
            OUT_ORDER += [("g", m_), ("t", m_ - 1)]
        OUT_ORDER.append(("t", KD - 1))

        block = ctx.enter_context(nc.Block())

        @block.sync
        def _(sp):
            sp.dma_start(consts[:, :], a["consts"]).then_inc(consts_in, 16)
            sp.dma_start(xtm[:, 0:TT, :], a["x_prompt"].rearrange("o (t p) d -> p (o t) d", p=P)).then_inc(x_in, 16)
            sp.dma_start(xtm[0:NB, TT, :], a["x_sample"].rearrange("b o d -> (b o) d")).then_inc(x_in, 16)
            wq = a["w_in"].rearrange("(k p) c -> p k c", p=P)
            slc = a["cache_kv_slc"].rearrange("n t k g d -> n t (k g d)")
            sp.wait_ge(pages_in, 16 * (1 + N_PAGES))
            for n, (kind, arg, count, _) in enumerate(PLAN):
                if count == 0:
                    continue
                if n >= NS:
                    sp.wait_ge(slab_used, n - NS + 1)
                S = slab(n)
                done = slab_in[n % NS]
                if kind == "win":
                    c0, w = arg
                    sp.dma_start(S[:, 0:KD * w].rearrange("p (k c) -> p k c", c=w),
                                 wq[:, :, c0:c0 + w]).then_inc(done, 16)
                elif kind == "q":
                    dst = S.rearrange("p (k h j d) -> p k h j d", k=KD, h=HPG, j=2)
                    for j in range(2):
                        for h in range(HPG):
                            c0 = ((2 * arg[0] + j) * HPG + h) * DH
                            sp.dma_start(dst[:, :, h, j, :], wq[:, :, c0:c0 + DH]).then_inc(done, 16)
                elif kind == "cmp":
                    for s_ in kv_store:
                        sp.wait_ge(s_, 16 * len(KV_TILES) // 4)
                    sp.dma_start(S[0:NCP + 1, :], a["kv_cmp_prompt"].rearrange(
                        "o (n f s) k g d -> f (o n) (s k g d)", f=2, s=8)[arg[1]]).then_inc(done, 16)
                elif kind == "winrows":
                    kv, bh = arg
                    dst = S.rearrange("p (b g c) -> p b g c", b=4, g=4)
                    for b4 in range(4):
                        src = a["state_kv_win"][4 * bh + b4].rearrange("(g t) k x d -> t k g (x d)", t=P)[:, kv]
                        sp.dma_start(dst[:, b4], src).then_inc(done, 16)
                elif kind in ("kpage", "vpage"):
                    kv = int(kind == "vpage")
                    dst = S.rearrange("p (x c) -> p x c", x=16)
                    for x in range(0, 16, 2):
                        at = slab_page(kind, arg, x)
                        v = sp.value_load(pages[0:1, at:at + 1], min_val=0, max_val=N_PHYS - 1)
                        sp.dma_start(dst[:, x, :], slc[bass.DynSlice(v, 1)].rearrange("o t c -> (o t) c")
                                     [:, 256 * kv:256 * kv + 256]).then_inc(done, 16)
                elif kind == "glu":
                    sp.dma_start(S[:, 0:2048].rearrange("p (k c) -> p k c", k=4),
                                 a["s5_w_glu"].rearrange("(k p) c -> p k c", p=P)).then_inc(done, 16)
                elif kind == "mix":
                    c0 = arg[0] * P
                    dst = S[:, 0:3 * D].rearrange("p (w k c) -> p w k c", w=3, c=P)
                    for w in range(2):
                        sp.dma_start(dst[:, w], wq[:, :, C_GM + w * D + c0:C_GM + w * D + c0 + P]).then_inc(done, 16)
                    wn = a["w_branch_nsa"].rearrange("(q j h d) c -> q j d h c", q=2, j=2, h=HPG)
                    for q in range(2):
                        for j in range(2):
                            sp.dma_start(dst[64 * j:64 * j + 64, 2, 4 * q:4 * q + 4, :],
                                         wn[q, j][:, :, c0:c0 + P]).then_inc(done, 16)
                    sp.dma_start(S[:, 3 * D:3 * D + 512].rearrange("p (k c) -> p k c", c=P),
                                 a["w_branch_s5"].rearrange("(k p) c -> p k c", p=P)[:, :, c0:c0 + P]
                                 ).then_inc(done, 16)
                elif kind == "out":
                    sp.dma_start(S.rearrange("p (k c) -> p k c", c=512),
                                 a["w_out"].rearrange("(k p) c -> p k c", p=P)[:, :, 512 * arg[0]:512 * arg[0] + 512]
                                 ).then_inc(done, 16)
                elif kind == "up":
                    sp.dma_start(S.rearrange("p (k c) -> p k c", c=512),
                                 a["w_mlp_up"].rearrange("(k p) c -> p k c", p=P)[:, :, 512 * arg[0]:512 * arg[0] + 512]
                                 ).then_inc(done, 16)
                elif kind == "down":
                    sp.dma_start(S.rearrange("p (k c) -> p k c", c=P),
                                 a["w_mlp_down"].rearrange("(k p) c -> p k c", p=P)[:, :, P * arg[0]:P * arg[0] + P]
                                 ).then_inc(done, 16)

        ROWS = [P] * TT + [NB]
        N_PAR = 14
        NORM_UNITS = [(t, half) for t in range(5) for half in range(2)]

        @block.gpsimd
        def _(pool):
            n_ch = [0]

            def link(ins):
                n_ch[0] += 1
                ins.then_inc(pool_ch, 1)
                pool.wait_ge(pool_ch, n_ch[0])

            pool.dma_start(a["kv_win_sample"][:, 0:WIN - 1].rearrange("b t k g d -> b (t k g d)"),
                           a["state_kv_win"][:, 1:WIN].rearrange("b t k g d -> b (t k g d)")).then_inc(copies, 16)
            nc.gpsimd.memset(R[:, 8192:12288], 0.0).then_inc(zero_ready, 1)
            nc.gpsimd.memset(R[:, 12288:16384], 0.0).then_inc(zero_ready, 1)
            pool.wait_ge(unit_ready, 1)
            pool.wait_ge(pair_free, 20)
            for grp in range(4):
                if grp >= 2:
                    pool.wait_ge(h_ready, 4 * (grp - 1))
                tr, ti = TAB[:, grp % 2, 0], TAB[:, grp % 2, 1]
                c = slice(4 * grp, 4 * grp + 4)
                nc.gpsimd.memset(tr[:, :, 0:1], 1.0)
                nc.gpsimd.memset(ti[:, :, 0:1], 0.0)
                nc.gpsimd.tensor_copy(ur[:, c], cs[:, c])
                link(nc.gpsimd.tensor_copy(ui[:, c], sn[:, c]))
                m = 1
                while m < T:
                    w = min(m, P)
                    for o in range(0, m, w):
                        Ur, Ui = (x[:, c].unsqueeze(2).to_broadcast([P, 4, w]) for x in (ur, ui))
                        Ar, Ai = (x[:, :, o:o + w] for x in (tr, ti))
                        Br, Bi = (x[:, :, m + o:m + o + w] for x in (tr, ti))
                        wk = WK[:, 0:4 * w].rearrange("p (i t) -> p i t", i=4)
                        nc.gpsimd.tensor_tensor(Br, Ar, Ur, ALU.mult)
                        link(nc.gpsimd.tensor_tensor(wk, Ai, Ui, ALU.mult))
                        link(nc.gpsimd.tensor_tensor(Br, Br, wk, ALU.subtract))
                        nc.gpsimd.tensor_tensor(Bi, Ar, Ui, ALU.mult)
                        link(nc.gpsimd.tensor_tensor(wk, Ai, Ur, ALU.mult))
                        link(nc.gpsimd.tensor_tensor(Bi, Bi, wk, ALU.add))
                    m *= 2
                    if m < T:
                        nc.gpsimd.tensor_tensor(tp0[:, c], ui[:, c], ui[:, c], ALU.mult)
                        link(nc.gpsimd.tensor_tensor(tp1[:, c], ur[:, c], ui[:, c], ALU.mult))
                        link(nc.gpsimd.tensor_tensor(ur[:, c], ur[:, c], ur[:, c], ALU.mult))
                        link(nc.gpsimd.tensor_tensor(ur[:, c], ur[:, c], tp0[:, c], ALU.subtract))
                        link(nc.gpsimd.tensor_tensor(ui[:, c], tp1[:, c], tp1[:, c], ALU.add))
                nc.gpsimd.tensor_copy(tp0[:, 0:1], ur[:, 0:1]).then_inc(table_ready, 1)
            pool.wait_ge(rows_ready, 1)
            cmp_rows = a["cache_kv_cmp"].rearrange("n (c s) k g d -> (n c) (s k g d)", s=8)
            slc_rows = a["cache_kv_slc"].rearrange("n t k g d -> (n t k) (g d)")
            for n, (kind, arg, _, count) in enumerate(PLAN):
                if count == 0:
                    continue
                pool.wait_ge(slab_used, n - NS + 1)
                if kind == "cmp":
                    b, half = arg
                    pool.indirect_dma_start(slab(n), None, cmp_rows, bass.IndirectOffsetOnAxis(
                        ap=row_cmp[:, half, b:b + 1], axis=0)).then_inc(rows_in[n % NS], 16)
                    continue
                kv = int(kind == "vpage")
                dst = slab(n).rearrange("p (x c) -> p x c", x=16)
                for x in range(1, 16, 2):
                    at = slab_page(kind, arg, x)
                    pool.indirect_dma_start(dst[:, x, :], None, slc_rows, bass.IndirectOffsetOnAxis(
                        ap=row_kv[:, kv, at:at + 1], axis=0)).then_inc(rows_in[n % NS], 16)
            pool.wait_ge(od_full, 1)
            nc.gpsimd.memset(KZ[64:128, 0, :, :], 0.0)
            nc.gpsimd.memset(KZ[0:64, 1, :, :], 0.0).then_inc(kz_ready, 1)
            for n, (t, p, h, j) in enumerate(TASKS):
                head = (2 * p + j) * HPG + h
                pool.wait_ge(as_rec, n + 1)
                for r in range(2):
                    k = 2 * (n % 2) + r
                    ins = nc.gpsimd.tensor_scalar(PP[:, n % 2, r, 0:P * (t + 1)], PP[:, n % 2, r, 0:P * (t + 1)],
                                                  ainv[:, k:k + 1], gtm[:, t, 3 * head + 1 + r:3 * head + 2 + r],
                                                  ALU.mult, ALU.mult)
                ins.then_inc(as_p, 1)
            pool.wait_ge(copies, 16)

        @block.scalar
        def _(act):
            n_ch = [0]

            def link(ins):
                n_ch[0] += 1
                ins.then_inc(act_ch, 1)
                act.wait_ge(act_ch, n_ch[0])

            def par(dst, src):
                act.dma_start(dst, src, allow_slow_non_contiguous=True).then_inc(par_in, 16)

            act.dma_start(pages[:, :], a["page_table"].rearrange("b (o n) -> o (b n)", o=1).to_broadcast(
                [P, NB * N_PAGES])).then_inc(pages_in, 16)
            for g in range(N_PAGES):
                act.dma_start(pages8[8 * g:8 * g + 8, :], a["page_table"].rearrange("b (o n) -> n o b", o=1)[g]
                              .to_broadcast([8, NB]), allow_slow_non_contiguous=True).then_inc(pages_in, 16)
            for w, name in enumerate(("norm_mix_pre", "norm_mlp_pre")):
                par(gT[:, w, :], a[name].rearrange("(k p) -> p k", p=P))
            for dst, name in ((are, "s5_a_re"), (aim, "s5_a_im")):
                for g in range(2):
                    par(dst[64 * g:64 * g + 64, :], a[name].rearrange("(i g) n -> g n i", g=2)[g])
            for g in range(2):
                par(ldt[64 * g:64 * g + 64, :],
                    a["s5_log_dt"].rearrange("(o i g) -> g o i", g=2, o=1)[g].to_broadcast([64, NST]))
            for r, name in enumerate(("s5_b_re", "s5_b_im")):
                for g in range(2):
                    par(bld[64 * g:64 * g + 64, r, :, :], a[name].rearrange("(i g) n c -> g n i c", g=2)[g])
            par(s5d[:, :], a["s5_d"].rearrange("(k p) -> p k", p=P))
            par(bglu[:, :], a["s5_b_glu"].rearrange("(k p) -> p k", p=P))
            act.dma_start(QO[0:NB, KD * NT:KD * NT + 4096],
                          a["state_s5"].rearrange("b g n r -> b (g n r)")).then_inc(h0_in, 16)

            def rms(src, junk_):
                for t, r in enumerate(ROWS):
                    link(nc.scalar.activation(junk_[0:r, :], src[0:r, t, :], ACT.Square,
                                              accum_out=ssq[0:r, t:t + 1]))
                nc.scalar.activation(ssq[:, 0:TT], ssq[:, 0:TT], ACT.Sqrt, scale=1.0 / D,
                                     bias=epsb[:, :])
                nc.scalar.activation(ssq[0:NB, TT:5], ssq[0:NB, TT:5], ACT.Sqrt, scale=1.0 / D,
                                     bias=epsb[0:NB, :]).then_inc(root_ready, 1)

            act.wait_ge(masks_ready, 1)
            act.wait_ge(x_in, 32)
            rms(xtm, junk)

            act.wait_ge(par_in, 16 * N_PAR)
            nc.scalar.activation(dt, ldt, ACT.Exp).then_inc(ldt_ready, 1)
            act.wait_ge(ang_ready, 1)
            nc.scalar.activation(mag, mag, ACT.Exp)
            nc.scalar.activation(sn, ang2, ACT.Sin)
            nc.scalar.activation(sh, ang2, ACT.Sin, scale=0.5).then_inc(trig_ready, 1)
            act.wait_ge(zero_ready, 2)
            for r, name in enumerate(("s5_c_re", "s5_c_im")):
                for ii in range(4):
                    for g in range(2):
                        row = 32 * ii + 16 * g
                        act.dma_start(CCP[row:row + C5, r, ii:NST:4, 64 * g:64 * g + 64],
                                      a[name].rearrange("(q i g) c n -> i g c q n", q=4, g=2)[ii, g]
                                      ).then_inc(c_in, 16)

            nkv = 0
            for u, unit in enumerate(HEAD_UNITS + REST_UNITS):
                act.wait_ge(pair_full, u + 1)
                kind = unit[0]
                pr = pair(u)
                if kind == "gemm" and unit[4][0] != "gn":
                    to = unit[4]
                    scale = 1.0
                    if to[0] == "u":
                        dst = uT[:, to[1], :]
                    elif to[0] == "q":
                        dst = qT[:, to[1], :]
                        scale = DH ** -0.5
                        if to[1] == 0:
                            for s_ in kv_store:
                                act.wait_ge(s_, 16 * len(KV_TILES) // 4)
                    elif to[1] > 0 and to[2] < 2:
                        dst = kT[:, 2 * (to[1] - 1) + to[2], :]
                    else:
                        dst = zst[:, to[2] % 2, :]
                    ins = nc.scalar.activation(halves(dst), pr[:, :, 0:HALF], ACT.Copy, scale=scale)
                elif kind == "gemm":
                    nc.scalar.activation(gsT[:, 0:HALF], pr[0:3 * NH, 0, 0:HALF], ACT.Sigmoid)
                    nc.scalar.activation(gsT[:, HALF:T], pr[0:3 * NH, 1, 0:T - HALF], ACT.Sigmoid)
                    ins = nc.scalar.activation(gsTs[0:3 * NH, :], pr[0:3 * NH, 1, T - HALF:HALF], ACT.Sigmoid)
                elif kind == "tr":
                    c, m = unit[1:]
                    if nkv >= 4:
                        act.wait_ge(kv_store[nkv % 4], 16 * (nkv // 4))
                    if c > 0 and m >= 2:
                        dst = vtm[:, :, 256 * (c - 1) + P * (m - 2):256 * (c - 1) + P * (m - 1)]
                    else:
                        dst = kst[:, nkv % 4]
                    nc.scalar.activation(kvs[:, KVW * c + P * m:KVW * c + P * m + P], pr[0:NB, 1, 0:P], ACT.Copy)
                    nc.scalar.activation(dst, pr[:, 0, :].rearrange("p (t c) -> p t c", t=TT),
                                         ACT.Copy).then_inc(pair_free, 1)
                    act.wait_ge(pair_free, u + 1)
                    name = ("kv_cmp_prompt", "kv_slc_prompt", "kv_win_prompt")[c]
                    out = a[name].rearrange("o (t p) k g d -> p (o t) (k g d)", p=P)[:, :, P * m:P * m + P]
                    act.dma_start(out, dst).then_inc(kv_store[nkv % 4], 16)
                    nkv += 1
                    continue
                elif kind == "trg":
                    nc.scalar.activation(gs8[0:NB, :], pr[0:NB, 1, 0:3 * NH], ACT.Copy)
                    ins = nc.scalar.activation(gtm[:, :, :],
                                               pr[:, 0, 0:TT * 3 * NH].rearrange("p (t c) -> p t c", t=TT), ACT.Copy)
                elif kind in ("bb", "cc"):
                    _, ri, q = unit
                    ins = nc.scalar.activation((BBT if kind == "bb" else CCT)[:, ri, 4 * q:4 * q + 4, :],
                                               pr[:, 0, :].rearrange("p (i c) -> p i c", i=4), ACT.Copy,
                                               scale=-1.0 if kind == "cc" and ri else 1.0)
                else:
                    ins = nc.scalar.activation(h0T if kind == "h0" else buS,
                                               pr[:, 0, 0:256].rearrange("p (i r b) -> p i r b", i=NST, r=2), ACT.Copy)
                ins.then_inc(pair_free, 1)

            for v in range(8):
                act.wait_ge(st_full, v + 1)
                src = PS[0:9, v % 2, :].rearrange("p (i r c) -> p i r c", i=2, r=2)
                for r in range(2):
                    ins = nc.scalar.activation(STO[:, 2 * v:2 * v + 2, :, r], src[:, :, r, :], ACT.Copy)
                ins.then_inc(st_ready, 1)
            act.wait_ge(st_ready, 8)
            flat = R[0:9, 8192:12288]
            act.dma_start(a["s5_prompt"].rearrange("b g n r -> b (g n r)"), flat[0:1]).then_inc(s5_store, 16)
            act.dma_start(a["s5_sample"].rearrange("b g n r -> b (g n r)"), flat[1:9]).then_inc(s5_store, 16)
            for c, name in enumerate(("kv_cmp_sample", "kv_slc_sample")):
                act.dma_start(a[name].rearrange("b o k g d -> (b o) (k g d)"),
                              kvs[:, KVW * c:KVW * c + KVW]).then_inc(stores, 16)
            act.dma_start(a["kv_win_sample"].rearrange("b t k g d -> b t (k g d)")[:, WIN - 1, :],
                          kvs[:, 2 * KVW:3 * KVW]).then_inc(stores, 16)
            act.wait_ge(s5_store, 32)
            act.wait_ge(y_free, 4)
            for k, kv in enumerate("kv"):
                w1 = a[f"cmp_w1_{kv}"].rearrange("(f s e) d h -> f e d s h", f=2, e=2)
                for f in range(2):
                    col = 64 * (f ^ k)
                    for e in range(2):
                        act.dma_start(w1c[64 * e:64 * e + 64, k, :, col:col + 64], w1[f, e]).then_inc(w1_in, 16)
                act.dma_start(w2[64 * k:64 * k + 64, :], a[f"cmp_w2_{kv}"]).then_inc(w1_in, 16)
                for e in range(2):
                    act.dma_start(peT[64 * e:64 * e + 64, k, :],
                                  a[f"cmp_pe_{kv}"].rearrange("(s e) d -> e d s", e=2)[e],
                                  allow_slow_non_contiguous=True).then_inc(w1_in, 16)
            def xt_evac(r, w):
                act.wait_ge(xt_full, r + 1)
                if r >= 3:
                    act.wait_ge(xt_used, r - 2)
                bank = 4 + r % 3 if r < N_RS else 6 + (r - N_RS) % 2
                nc.scalar.activation(XT[:, r % 3, 0:w], PS[:, bank, 0:w], ACT.Copy).then_inc(xt_ready, 1)

            def gelu(b):
                w = 4 * (NC if b < NB else NCP)
                act.wait_ge(pre_ready, b + 1)
                if b:
                    act.wait_ge(l2_full, b)
                nc.scalar.activation(GEL[:, 0:w], PRE[:, 0:w], ACT.Gelu_apprx_tanh).then_inc(gelu_ready, 1)

            for r, (b, half, kind, s4) in enumerate(RS):
                xt_evac(r, 4 * (NCH if b < NB else NCP + 1))
                if b and r % 16 == 3:
                    gelu(b - 1)
            gelu(NB)
            act.wait_ge(l2_full, NB + 1)
            act.dma_start(R[0:32, 2625:3714], a["tie"].rearrange("p j i -> p (j i)")).then_inc(tie_in, 16)

            for r in range(len(KR)):
                xt_evac(N_RS + r, 512)
                if r == 15:
                    act.wait_ge(sc_max, 1)
                    nc.scalar.activation(SC[:, 0:NC], SC[:, 0:NC], ACT.Exp, bias=dmx[:, 0:1],
                                         accum_out=dsm[:, 0:1]).then_inc(sc_exp, 1)
            act.wait_ge(smax, 1)
            nc.scalar.activation(SA, SA, ACT.Exp, bias=dmx[:, 1:2], accum_out=dsm[:, 1:2])
            nc.scalar.activation(SW[:, 1:513], SW[:, 1:513], ACT.Exp, bias=dmx[:, 2:3],
                                 accum_out=dsm[:, 2:3]).then_inc(sexp, 1)
            for v in range(6):
                act.wait_ge(pt_full, v + 1)
                bank = 2 + v % 4
                if v < 5:
                    ins = nc.scalar.activation(PTA[:, 4 * v:4 * v + 4, :],
                                               PS[:, bank, :].rearrange("p (g c) -> p g c", g=4), ACT.Copy)
                else:
                    nc.scalar.activation(PTC[0:NC, :], PS[0:NC, bank, 0:P], ACT.Copy)
                    ins = nc.scalar.activation(PTN, PS[0:NB, bank, P:3 * P].rearrange("p (r c) -> p r c", r=2),
                                               ACT.Copy)
                ins.then_inc(pt_ready, 1)

            act.wait_ge(od_full, 1)
            for j in range(2):
                ins = nc.scalar.activation(KZ[64 * j:64 * j + 64, j], kT[64 * j:64 * j + 64, :, 0:T], ACT.Copy)
            ins.then_inc(kz_ready, 1)
            for t in range(TT):
                act.wait_ge(cs_max, t + 1)
                nc.scalar.activation(PCP[:, t], PCP[:, t], ACT.Exp).then_inc(cs_exp, 1)
            for n in range(NTK + 1):
                if n < NTK:
                    t = TASKS[n][0]
                    act.wait_ge(as_max, n + 1)
                    if n >= 2:
                        act.wait_ge(at_full, n - 1)
                    for r in range(2):
                        k = 2 * (n % 2) + r
                        ins = nc.scalar.activation(PP[:, n % 2, r, 0:P * (t + 1)],
                                                   PS[:, 1 + k, 0:P * (t + 1)], ACT.Exp,
                                                   bias=amx[:, k:k + 1], accum_out=asm[:, k:k + 1])
                    ins.then_inc(as_exp, 1)
                if n >= 1:
                    m = n - 1
                    t = TASKS[m][0]
                    act.wait_ge(at_full, m + 1)
                    if m >= 2:
                        act.wait_ge(ao_full, m - 1)
                    nc.scalar.activation(PTP[:, m % 2, 0:t + 1, :],
                                         PS[:, 5, 0:P * (t + 1)].rearrange("p (g c) -> p g c", c=P),
                                         ACT.Copy).then_inc(at_a, 1)

            act.wait_ge(ao_free, NTK)
            for q in range(4):
                ins = nc.scalar.activation(zT[:, q, :], uT[:, q, :], ACT.Gelu_apprx_tanh)
            ins.then_inc(z_ready, 1)
            for m in range(4):
                u = U_GLU + m
                act.wait_ge(pair_full, u + 1)
                if m >= 2:
                    act.wait_ge(os5_ready, m - 1)
                nc.scalar.activation(halves(sgl[:, m % 2, :]), pair(u)[:, :, 0:HALF], ACT.Sigmoid,
                                     bias=bglu[:, m:m + 1]).then_inc(pair_free, 1)
            for m in range(KD):
                for w in range(4):
                    u = U_MIX + 4 * m + w
                    act.wait_ge(pair_full, u + 1)
                    if m >= 2 and w == 0:
                        act.wait_ge(mix_ready, m - 1)
                    nc.scalar.activation(halves(mxb[:, m % 2, w, :]), pair(u)[:, :, 0:HALF],
                                         ACT.Sigmoid if w < 2 else ACT.Copy).then_inc(pair_free, 1)

            act.dma_start(x1[:, 0:TT, :], a["x_prompt"].rearrange("o (t p) d -> p (o t) d", p=P)).then_inc(x2_in, 16)
            act.dma_start(x1[0:NB, TT, :], a["x_sample"].rearrange("b o d -> (b o) d")).then_inc(x2_in, 16)
            act.dma_start(gain, a["norm_mix_post"].rearrange("(o d) -> o d", o=1).to_broadcast([P, D])
                          ).then_inc(gain_in, 16)

            def out_units(base, stage):
                for i, (kind, m) in enumerate(OUT_ORDER):
                    u = base + i
                    act.wait_ge(pair_full, u + 1)
                    pr = pair(u)
                    if kind == "g":
                        ins = nc.scalar.activation(halves(stage[:, m % 2, :]), pr[:, :, 0:HALF], ACT.Copy)
                    else:
                        nc.scalar.activation(ytm[0:NB, TT, P * m:P * m + P], pr[0:NB, 1, 0:P], ACT.Copy)
                        ins = nc.scalar.activation(ytm[:, 0:TT, P * m:P * m + P],
                                                   pr[:, 0, :].rearrange("p (t c) -> p t c", t=TT), ACT.Copy)
                    ins.then_inc(pair_free, 1)
                act.wait_ge(pair_free, base + len(OUT_ORDER))

            out_units(U_OUT, zo)
            rms(ytm, xn2[:, 0, :])
            act.wait_ge(x1_ready, 5)
            act.dma_start(gain, a["norm_mlp_post"].rearrange("(o d) -> o d", o=1).to_broadcast([P, D])
                          ).then_inc(gain_in, 16)
            rms(x1, xn2[:, 0, :])
            for m in range(KF):
                u = U_UP + m
                act.wait_ge(pair_full, u + 1)
                nc.scalar.activation(halves(fT[:, m, :]), pair(u)[:, :, 0:HALF], ACT.Relu).then_inc(pair_free, 1)
            out_units(U_DOWN, hT)
            rms(ytm, xn2[:, 0, :])
            for t in range(5):
                act.wait_ge(x1_ready, 6 + t)
                if t < TT:
                    act.dma_start(a["y_prompt"][0, P * t:P * t + P, :], x1[:, t, :]).then_inc(stores, 16)
                else:
                    act.dma_start(a["y_sample"].rearrange("b o d -> (b o) d"), x1[0:NB, TT, :]).then_inc(stores, 16)
            act.wait_ge(stores, 16 * 8)

        @block.vector
        def _(dve):
            n_ch = [0]

            def link(ins):
                n_ch[0] += 1
                ins.then_inc(dve_ch, 1)
                dve.wait_ge(dve_ch, n_ch[0])

            V = nc.vector
            V.memset(epsb, EPS)
            dve.wait_ge(consts_in, 16)
            V.tensor_copy(idb[:, :], ident)
            V.tensor_copy(maskb[:, :], consts[:, CO_MASK:CO_MASK + P]).then_inc(masks_ready, 1)

            def pre_norm(first, src, dst, gains, which):
                dve.wait_ge(root_ready, which + 1)
                link(V.reciprocal(rstd[:, 0:TT], ssq[:, 0:TT]))
                link(V.reciprocal(rstd[0:NB, TT:5], ssq[0:NB, TT:5]))

                def evac(t):
                    for half in range(2):
                        v = first + 2 * t + half
                        w = ROWS[t]
                        dve.wait_ge(xnt_full, v + 1)
                        V.tensor_tensor(hT[:, 4 * half:4 * half + 4, P * t:P * t + w],
                                        PS[:, 4 + v % 4, 0:4 * w].rearrange("p (k c) -> p k c", k=4),
                                        gains[:, 4 * half:4 * half + 4].unsqueeze(2).to_broadcast([P, 4, w]),
                                        ALU.mult).then_inc(xnt_free, 1)

                for t, r in enumerate(ROWS):
                    if t >= 2:
                        dve.wait_ge(xnt_full, first + 2 * (t - 1))
                    V.tensor_scalar(dst[0:r, t % 2, :], src[0:r, t, :], rstd[0:r, t:t + 1], None,
                                    ALU.mult).then_inc(xn_ready, 1)
                    if t:
                        evac(t - 1)
                evac(4)

            dve.wait_ge(par_in, 16 * N_PAR)
            pre_norm(0, xtm, xn, gT[:, 0, :], 0)

            dve.wait_ge(pages_in, 16 * (1 + N_PAGES))
            link(V.tensor_scalar(row_kv[:, 0], pages[:, :], 2.0 * PAGE, consts[:, CO_ROW:CO_ROW + 1], ALU.mult, ALU.add))
            V.tensor_scalar(row_kv[:, 1], row_kv[:, 0], 1.0, None, ALU.add)
            link(V.tensor_scalar(row_cmp[:, 0], pages8[:, :], 16.0, consts[:, CO_ROW + 1:CO_ROW + 2],
                                 ALU.mult, ALU.add))
            V.tensor_scalar(row_cmp[:, 1], row_cmp[:, 0], 1.0, None, ALU.add).then_inc(rows_ready, 1)

            dve.wait_ge(ldt_ready, 1)
            V.tensor_tensor(mag, are, dt, ALU.mult)
            link(V.tensor_tensor(ang, aim, dt, ALU.mult))
            link(V.tensor_scalar(s5t, ang, 1.0 / TWO_PI, None, ALU.mult))
            link(V.tensor_scalar(s5t, s5t, RND, RND, ALU.add, ALU.subtract))
            link(V.scalar_tensor_tensor(ang2, s5t, -6.28125, ang, ALU.mult, ALU.add))
            link(V.scalar_tensor_tensor(ang2, s5t, -(TWO_PI - 6.28125), ang2, ALU.mult, ALU.add))
            V.tensor_scalar(ang2, ang2, 3.1415925, -3.1415925, ALU.min, ALU.max).then_inc(ang_ready, 1)
            dve.wait_ge(trig_ready, 1)
            link(V.tensor_tensor(s5t, sh, sh, ALU.mult))
            link(V.tensor_scalar(cs, s5t, -2.0, 1.0, ALU.mult, ALU.add))
            link(V.tensor_tensor(abr, mag, cs, ALU.mult))
            link(V.tensor_tensor(abi, mag, sn, ALU.mult))
            V.tensor_scalar(nabi, abi, -1.0, None, ALU.mult).then_inc(unit_ready, 1)
            link(V.tensor_tensor(den, are, are, ALU.mult))
            link(V.tensor_tensor(s5t, aim, aim, ALU.mult))
            link(V.tensor_tensor(den, den, s5t, ALU.add))
            link(V.reciprocal(den, den))
            link(V.tensor_scalar(s5u, abr, -1.0, None, ALU.add))
            link(V.tensor_tensor(cor, s5u, are, ALU.mult))
            link(V.tensor_tensor(s5t, abi, aim, ALU.mult))
            link(V.tensor_tensor(cor, cor, s5t, ALU.add))
            link(V.tensor_tensor(cor, cor, den, ALU.mult))
            link(V.tensor_tensor(coi, abi, are, ALU.mult))
            link(V.tensor_tensor(s5t, s5u, aim, ALU.mult))
            link(V.tensor_tensor(coi, coi, s5t, ALU.subtract))
            link(V.tensor_tensor(coi, coi, den, ALU.mult))
            CR, CI = (x.unsqueeze(2).to_broadcast([P, NST, C5]) for x in (cor, coi))
            V.tensor_tensor(bwk[:, 0], bld[:, 0], CR, ALU.mult)
            V.tensor_tensor(bwk[:, 1], bld[:, 1], CI, ALU.mult)
            V.tensor_tensor(bwk[:, 2], bld[:, 0], CI, ALU.mult)
            link(V.tensor_tensor(bwk[:, 3], bld[:, 1], CR, ALU.mult))
            dve.wait_ge(zero_ready, 1)
            for r, op in ((0, ALU.subtract), (1, ALU.add)):
                for ii in range(4):
                    for g in range(2):
                        rows, col = slice(64 * g, 64 * g + 64), 32 * ii + 16 * g
                        ins = V.tensor_tensor(BBP[rows, r, ii:NST:4, col:col + C5], bwk[rows, 2 * r, ii:NST:4, :],
                                              bwk[rows, 2 * r + 1, ii:NST:4, :], op)
            ins.then_inc(bb_ready, 1)

            def y_evac(q):
                dve.wait_ge(y_full, q + 1)
                V.scalar_tensor_tensor(uT[:, q, 0:T], uT[:, q, 0:T], s5d[:, q:q + 1], PS[:, 6, 0:T],
                                       ALU.mult, ALU.add)
                V.scalar_tensor_tensor(uT[:, q, T:NT], uT[:, q, T:NT], s5d[:, q:q + 1], PS[:, 7, 0:NB],
                                       ALU.mult, ALU.add).then_inc(y_free, 1)

            t1, t2, xr, xi = (w[:, 0:T] for w in W5[0:4])
            for i in range(NST):
                if i % 4 == 0:
                    dve.wait_ge(table_ready, i // 4 + 1)
                if i == 0:
                    dve.wait_ge(pair_free, 22)
                ct, st = TAB[:, (i // 4) % 2, 0, i % 4, :], TAB[:, (i // 4) % 2, 1, i % 4, :]
                hr, hi = W5[4 + 2 * (i % 2)], W5[5 + 2 * (i % 2)]
                dve.wait_ge(bu_full, i + 1)
                br, bi = PS[:, 4, :], PS[:, 5, :]
                V.tensor_tensor(t1, br, ct, ALU.mult)
                link(V.tensor_tensor(t2, bi, st, ALU.mult))
                V.tensor_tensor(xr, t1, t2, ALU.add)
                link(V.tensor_tensor(xi, bi, ct, ALU.mult))
                V.tensor_tensor(t2, br, st, ALU.mult).then_inc(bu_free, 1)
                dve.wait_ge(bu_free, i + 1)
                r = mag[:, i:i + 1].to_broadcast([P, T])
                link(V.tensor_tensor(xi, xi, t2, ALU.subtract))
                V.tensor_tensor_scan(xr, r, xr, 0.0, ALU.mult, ALU.add)
                link(V.tensor_tensor_scan(xi, r, xi, 0.0, ALU.mult, ALU.add))
                if i >= 2:
                    dve.wait_ge(h_used, i - 1)
                V.tensor_tensor(hr[:, 0:T], ct, xr, ALU.mult)
                link(V.tensor_tensor(t2, st, xi, ALU.mult))
                V.tensor_tensor(hr[:, 0:T], hr[:, 0:T], t2, ALU.subtract)
                V.tensor_tensor(hi[:, 0:T], st, xr, ALU.mult)
                link(V.tensor_tensor(t1, ct, xi, ALU.mult))
                V.tensor_tensor(hi[:, 0:T], hi[:, 0:T], t1, ALU.add)
                V.scalar_tensor_tensor(sst[:, 0], h0T[:, i, 0], abr[:, i:i + 1], buS[:, i, 0], ALU.mult, ALU.add)
                link(V.scalar_tensor_tensor(sst[:, 1], h0T[:, i, 1], abr[:, i:i + 1], buS[:, i, 1],
                                            ALU.mult, ALU.add))
                V.scalar_tensor_tensor(hr[:, T:NT], h0T[:, i, 1], nabi[:, i:i + 1], sst[:, 0], ALU.mult, ALU.add)
                link(V.scalar_tensor_tensor(hi[:, T:NT], h0T[:, i, 0], abi[:, i:i + 1], sst[:, 1],
                                            ALU.mult, ALU.add))
                V.tensor_copy(hS[:, i, 0], hr[:, T - 1:NT])
                V.tensor_copy(hS[:, i, 1], hi[:, T - 1:NT]).then_inc(h_ready, 1)
                if i % 4 == 0 and i:
                    y_evac(i // 4 - 1)
            y_evac(3)

            dve.wait_ge(pos_full, 1)
            V.tensor_copy(pos[0:64], PS[0:64, 7, 0:1])
            link(V.tensor_copy(pos[64:128], PS[0:64, 7, 1:2]))
            def permute(w):
                b, half, kind = w // 4, w // 2 % 2, w % 2
                n = NCH if b < NB else NCP + 1
                s = SLAB[("cmp", (b, half))]
                if kind == 0:
                    wait_slab(dve, s)
                if w >= 3:
                    dve.wait_ge(xt_full, 4 * (w - 2))
                V.tensor_copy(ROWSP[0:n, w % 3], slab(s)[0:n].rearrange("p (s k g d) -> p k g s d", s=8, k=2, g=4)
                              [:, kind]).then_inc(perm_ready, 1)

            for w in range(4):
                permute(w)
            for b in range(NB + 1):
                if b < NB:
                    permute(4 * b + 4)
                    permute(4 * b + 5)
                n = NCH if b < NB else NCP + 1
                k4 = PS[:, 2 * (b % 2), 0:4 * n].rearrange("p (g n) -> p g n", g=4)
                v4 = PS[:, 2 * (b % 2) + 1, 0:4 * n].rearrange("p (g n) -> p g n", g=4)
                sh4 = SH[:, 0:4 * n].rearrange("p (g n) -> p g n", g=4)
                pr4 = PRE[:, 0:4 * (n - 1)].rearrange("p (g n) -> p g n", g=4)
                dve.wait_ge(acc_full, b + 1)
                V.tensor_copy(SH[0:64, 0:4 * n], PS[64:128, 2 * (b % 2), 0:4 * n])
                link(V.tensor_copy(SH[64:128, 0:4 * n], PS[0:64, 2 * (b % 2) + 1, 0:4 * n]))
                if b:
                    dve.wait_ge(gelu_ready, b)
                for rows, acc in ((slice(0, 64), k4), (slice(64, 128), v4)):
                    ins = V.scalar_tensor_tensor(pr4[rows], acc[rows][:, :, 0:n - 1], pos[rows, 0:1],
                                                 sh4[rows][:, :, 1:n], ALU.add, ALU.add)
                ins.then_inc(pre_ready, 1)
                if b < NB:
                    permute(4 * b + 6)
                dve.wait_ge(l2_full, b + 1)
                for j in range(2):
                    V.tensor_copy(kcT[64 * j:64 * j + 64, b, :, 0:n - 1],
                                  PS[0:64, 2 * (b % 2), 0:4 * (n - 1)].rearrange("p (q j n) -> p q j n", q=2, j=2)
                                  [:, :, j, :])
                if b == NB:
                    link(V.memset(KCZ, 0.0))
                    for j in range(2):
                        V.tensor_copy(KCZ[64 * j:64 * j + 64, :, j, :],
                                      PS[0:64, 2 * (b % 2), 0:4 * NCP].rearrange("p (q j n) -> p q j n", q=2, j=2)
                                      [:, :, j, :])
                V.tensor_copy(vc[0:n - 1, b, :], PS[0:n - 1, 2 * (b % 2) + 1, 0:256]).then_inc(l2_ready, 1)
                if b < NB:
                    permute(4 * b + 7)
                else:
                    link(V.memset(QP[:, :, :, :], 0.0))
                    for p in range(2):
                        flat = QP[:, p].rearrange("p b c -> p (b c)")
                        for j in range(2):
                            for h in range(HPG):
                                c0 = 8 * p + 4 * j + h
                                ins = V.tensor_copy(flat[64 * j:64 * j + 64, c0:c0 + 144 * 7 + 1:144],
                                                    qT[64 * j:64 * j + 64, 4 * p + h, T:NT])
                    ins.then_inc(qpad_ready, 1)

            dve.wait_ge(sc_full, 1)
            V.tensor_tensor(GH.rearrange("p (h r) -> p h r", r=3),
                            PS[:, 4, 0:48].rearrange("p (h r) -> p h r", r=3),
                            consts[:, CO_HM:CO_HM + NH].unsqueeze(2).to_broadcast([P, NH, 3]), ALU.mult)
            link(V.tensor_copy(SC, PS[:, 5, 0:129]))
            V.tensor_reduce(gd, GH.rearrange("p (h r) -> p r h", r=3), AX, ALU.add)
            V.reduce_max(dmx[:, 0:1], SC[:, 0:NC], AX, negate=True).then_inc(sc_max, 1)
            dve.wait_ge(sc_exp, 1)
            link(V.reciprocal(dinv[:, 0:1], dsm[:, 0:1]))
            V.tensor_scalar(SC[:, 0:NC], SC[:, 0:NC], dinv[:, 0:1], None, ALU.mult).then_inc(pc_ready, 1)
            link(V.memset(IMP, 0.0))
            dve.wait_ge(imp_full, 1)
            link(V.tensor_copy(IMP[:, 1:NC + 1], PS[0:32, 5, 0:NC]))
            link(V.tensor_reduce(SSEL, IMP[:, 0:132].rearrange("p (j k) -> p j k", k=4), AX, ALU.add))
            link(V.tensor_tensor(SSEL, SSEL, IMP[:, 4:133:4], ALU.add))
            V.memset(SSEL[:, 0:1], FORCE)
            link(V.memset(SSEL[:, NSEL - 2:NSEL], FORCE))
            Si = SSEL.unsqueeze(1).to_broadcast([32, NSEL, NSEL])
            Sj = SSEL.unsqueeze(2).to_broadcast([32, NSEL, NSEL])
            dve.wait_ge(tie_in, 16)
            V.tensor_tensor(CMPA, Si, Sj, ALU.is_gt)
            link(V.tensor_tensor(CMPB, Si, Sj, ALU.is_equal))
            link(V.tensor_tensor(CMPB, CMPB, TIE, ALU.mult))
            link(V.tensor_tensor(CMPA, CMPA, CMPB, ALU.add))
            link(V.tensor_reduce(SSEL, CMPA, AX, ALU.add))
            V.tensor_scalar(SSEL, SSEL, float(TOPK), None, ALU.is_lt).then_inc(sel_ready, 1)
            dve.wait_ge(selx_full, 1)
            link(V.tensor_scalar(SELX, PS[:, 5, 0:NSEL], 1.0, -NEG, ALU.subtract, ALU.mult))
            for q in range(4):
                dve.wait_ge(s_full, q + 1)
                V.tensor_tensor(SA[:, 512 * q:512 * q + 512].rearrange("p (j t) -> p j t", t=SELB),
                                PS[:, q, :].rearrange("p (j t) -> p j t", t=SELB),
                                SELX[:, 8 * q:8 * q + 8].unsqueeze(2).to_broadcast([P, 8, SELB]), ALU.add)
            V.tensor_tensor(SA[:, 2048:2049], SC[:, NC:NC + 1], SELX[:, NSEL - 1:NSEL], ALU.add)
            dve.wait_ge(s_full, 5)
            V.tensor_copy(SW[:, 512:513], SC[:, NC + 1:NC + 2])
            link(V.tensor_copy(SW[:, 0:512], PS[:, 4, :]))
            V.reduce_max(dmx[:, 2:3], SW[:, 1:513], AX, negate=True)
            V.reduce_max(dmx[:, 1:2], SA, AX, negate=True).then_inc(smax, 1)
            dve.wait_ge(sexp, 1)
            link(V.reciprocal(dinv[:, 1:3], dsm[:, 1:3]))
            link(V.tensor_tensor(dinv[:, 1:3], dinv[:, 1:3], gd[:, 1:3], ALU.mult))
            V.tensor_scalar(SC[:, 0:NC], SC[:, 0:NC], gd[:, 0:1], None, ALU.mult)
            V.memset(SW[:, 0:1], 0.0)
            V.tensor_scalar(SA, SA, dinv[:, 1:2], None, ALU.mult)
            link(V.tensor_scalar(SW[:, 1:513], SW[:, 1:513], dinv[:, 2:3], None, ALU.mult))
            V.tensor_scalar(PNB[:, 0], consts[:, CO_BM:CO_BM + NB], SA[:, 2048:2049], None, ALU.mult)
            V.tensor_scalar(PNB[:, 1], consts[:, CO_BM:CO_BM + NB], SW[:, 512:513], None,
                            ALU.mult).then_inc(p_ready, 1)
            dve.wait_ge(od_full, 1)
            own = consts[0:NH, CO_GM16:CO_GM16 + 4 * NB].unsqueeze(2).to_broadcast([NH, 4 * NB, DH])
            V.tensor_tensor(OD, PS[0:NH, 0:4, :].rearrange("p b (x d) -> p (b x) d", d=DH), own, ALU.mult)
            V.tensor_tensor(OE, PS[0:NH, 4:8, :].rearrange("p b (x d) -> p (b x) d", d=DH), own,
                            ALU.mult).then_inc(od_ready, 1)
            dve.wait_ge(od_ready, 1)
            link(V.tensor_tensor(OD, OD, OE, ALU.add))
            V.tensor_reduce(OS, OD.rearrange("p (b g) d -> p b d g", g=NG), AX, ALU.add).then_inc(ot_ready, 1)

            for t in range(TT):
                dve.wait_ge(cs_full, t + 1)
                for j in range(2):
                    ins = V.tensor_tensor(PCP[:, t].rearrange("p (q j h) n -> p j q h n", q=2, j=2)[:, j],
                                          PS[:, t, 0:NH * NCP].rearrange("p (q h j n) -> p j q h n", q=2, h=HPG, j=2)
                                          [:, j],
                                          consts[:, CO_CMASK + NCP * t:CO_CMASK + NCP * (t + 1)].unsqueeze(1)
                                          .unsqueeze(1).to_broadcast([P, 2, HPG, NCP]), ALU.add)
                link(ins)
                link(V.reduce_max(cmx, PCP[:, t], AX))
                V.tensor_tensor(PCP[:, t], PCP[:, t], cmx.unsqueeze(2).to_broadcast([P, NH, NCP]),
                                ALU.subtract).then_inc(cs_max, 1)
                dve.wait_ge(cs_exp, t + 1)
                link(V.reduce_sum(csm, PCP[:, t], AX))
                link(V.reciprocal(csm, csm))
                link(V.scalar_tensor_tensor(csm, csm, consts[:, CO_ROWV + t:CO_ROWV + t + 1],
                                            gtm[:, t, 0:3 * NH:3], ALU.mult, ALU.mult))
                link(V.tensor_tensor(PCP[:, t], PCP[:, t], csm.unsqueeze(2).to_broadcast([P, NH, NCP]), ALU.mult))
            dve.wait_ge(ot_full, 1)
            for p in range(2):
                for j in range(2):
                    ins = V.tensor_copy(oT[64 * j:64 * j + 64, 4 * p:4 * p + 4, T:NT],
                                        PS[0:DH, 4, 0:P].rearrange("p (b x) -> p x b", x=NH)
                                        [:, 8 * p + 4 * j:8 * p + 4 * j + 4, :])
            ins.then_inc(cs_done, 1)
            for n in range(NTK + 2):
                if n < NTK:
                    t = TASKS[n][0]
                    dve.wait_ge(as_full, n + 1)
                    for r in range(2):
                        k = 2 * (n % 2) + r
                        ins = V.reduce_max(amx[:, k:k + 1], PS[:, 1 + k, 0:P * (t + 1)], AX, negate=True)
                    ins.then_inc(as_max, 1)
                if 1 <= n <= NTK:
                    m = n - 1
                    t = TASKS[m][0]
                    dve.wait_ge(at_full, m + 1)
                    if m >= 2:
                        dve.wait_ge(ao_full, m - 1)
                    V.tensor_copy(PTPC[0:NCP, m % 2, :], PS[0:NCP, 0, 0:P])
                    V.tensor_copy(PTP[:, m % 2, 4:5 + t, :],
                                  PS[:, 6, 0:P * (t + 1)].rearrange("p (g c) -> p g c", c=P)).then_inc(at_d, 1)
                if n >= 2:
                    t, p, h, j = TASKS[n - 2]
                    dve.wait_ge(ao_full, n - 1)
                    V.tensor_copy(oT[64 * j:64 * j + 64, 4 * p + h, P * t:P * t + P],
                                  PS[0:64, 7, 0:P]).then_inc(ao_free, 1)
                if n < NTK:
                    dve.wait_ge(as_exp, n + 1)
                    k = 2 * (n % 2)
                    V.reciprocal(ainv[:, k:k + 2], asm[:, k:k + 2]).then_inc(as_rec, 1)

            for m in range(4):
                dve.wait_ge(pair_free, U_GLU + m + 1)
                V.tensor_tensor(uT[:, m, :], zT[:, m, :], sgl[:, m % 2, :], ALU.mult).then_inc(os5_ready, 1)
            for m in range(KD):
                dve.wait_ge(pair_free, U_MIX + 4 * m + 4)
                A, B, N_, S_ = (mxb[:, m % 2, w, :] for w in range(4))
                V.tensor_tensor(A, A, N_, ALU.mult)
                link(V.tensor_tensor(B, B, S_, ALU.mult))
                V.tensor_tensor(mT[:, m, :], A, B, ALU.add).then_inc(mix_ready, 1)

            def post_norm(which, roots):
                dve.wait_ge(root_ready, roots + 1)
                dve.wait_ge(gain_in, 16 * (which + 1))
                V.reciprocal(rstd[:, 0:TT], ssq[:, 0:TT])
                link(V.reciprocal(rstd[0:NB, TT:5], ssq[0:NB, TT:5]))
                for t, r in enumerate(ROWS):
                    link(V.scalar_tensor_tensor(ytm[0:r, t, :], ytm[0:r, t, :], rstd[0:r, t:t + 1], gain[0:r, :],
                                                ALU.mult, ALU.mult))
                    V.tensor_tensor(x1[0:r, t, :], x1[0:r, t, :], ytm[0:r, t, :], ALU.add).then_inc(x1_ready, 1)

            dve.wait_ge(x2_in, 32)
            post_norm(0, 1)
            pre_norm(10, x1, xn2, gT[:, 1, :], 2)
            for m in range(KF):
                dve.wait_ge(pair_free, U_UP + m + 1)
                V.tensor_tensor(fT[:, m, :], fT[:, m, :], fT[:, m, :], ALU.mult).then_inc(f_ready, 1)
            post_norm(1, 3)

        @block.tensor
        def _(pe):
            M = nc.tensor.matmul

            def tp(out, in_, rows=P):
                return nc.tensor.transpose(out, in_, ident[0:rows, 0:rows])

            def norm_transposes(first, src):
                for v0, (t, half) in enumerate(NORM_UNITS):
                    v = first + v0
                    r = ROWS[t]
                    pe.wait_ge(xn_ready, first // 2 + t + 1)
                    if v >= 4:
                        pe.wait_ge(xnt_free, v - 3)
                    for k in range(4):
                        ins = tp(PS[:, 4 + v % 4, r * k:r * k + r],
                                 src[0:r, t % 2, P * (4 * half + k):P * (4 * half + k) + P], r)
                    ins.then_inc(xnt_full, 1)

            def open_pair(u):
                if u >= 2:
                    pe.wait_ge(pair_free, u - 1)

            def gemm(u, lhs, rhs, w=P):
                n = len(lhs)
                for hf in range(2):
                    for k in range(n):
                        ins = M(pair(u)[0:w, hf, 0:HALF], lhs[k], rhs[k][:, HALF * hf:HALF * hf + HALF],
                                start=(k == 0), stop=(k == n - 1))
                return ins

            def back(u, src, w=P):
                for t in range(TT):
                    tp(pair(u)[:, 0, w * t:w * t + w], src[0:w, P * t:P * t + P], w)
                return tp(pair(u)[0:NB, 1, 0:w], src[0:w, T:NT], w)

            pe.wait_ge(consts_in, 16)
            norm_transposes(0, xn)
            pe.wait_ge(xnt_free, 10)

            last_of = {}
            for u, unit in enumerate(HEAD_UNITS + REST_UNITS):
                if unit[0] == "gemm":
                    last_of[SLAB[unit[1]]] = u

            def projection(u, unit):
                open_pair(u)
                kind = unit[0]
                pr = pair(u)
                if kind == "gemm":
                    _, key, m, w, to = unit
                    n = SLAB[key]
                    wait_slab(pe, n)
                    width = 512 if w == P else w
                    S = slab(n)[:, 0:KD * width].rearrange("p (k c) -> p k c", c=width)
                    ins = gemm(u, [S[:, k, P * m:P * m + w] for k in range(KD)], [hT[:, k, :] for k in range(KD)], w)
                    ins.then_inc(pair_full, 1)
                    if last_of[n] == u:
                        pe.wait_ge(pair_full, u + 1)
                        pe.sem_inc(slab_used, 1)
                    return
                if kind == "tr":
                    c, m = unit[1:]
                    src = kT[:, 2 * (c - 1) + m, :] if c > 0 and m < 2 else zst[:, m % 2, :]
                    ins = back(u, src)
                elif kind == "trg":
                    for t in range(TT):
                        tp(pr[:, 0, 48 * t:48 * t + 48], gsT[:, P * t:P * t + P], 48)
                    ins = tp(pr[0:NB, 1, 0:48], gsTs[0:48, :], 48)
                elif kind == "bb":
                    _, ri, q = unit
                    pe.wait_ge(bb_ready, 1)
                    for i in range(4):
                        ins = tp(pr[:, 0, P * i:P * i + P], BBP[:, ri, 4 * q + i, :])
                elif kind == "cc":
                    _, ri, q = unit
                    pe.wait_ge(c_in, 16 * 16)
                    for i in range(4):
                        ins = tp(pr[:, 0, P * i:P * i + P], CCP[:, ri, 4 * q + i, :])
                elif kind == "h0":
                    pe.wait_ge(h0_in, 16)
                    for i in range(NST):
                        for r in range(2):
                            ins = tp(pr[:, 0, 16 * i + 8 * r:16 * i + 8 * r + 8], st0[:, i, r, :], NB)
                else:
                    pe.wait_ge(pair_free, u - 1)
                    for i in range(NST):
                        for r in range(2):
                            ins = M(pr[:, 0, 16 * i + 8 * r:16 * i + 8 * r + 8], BBT[:, r, i, :],
                                    uT[:, i // 4, T:NT], start=True, stop=True)
                ins.then_inc(pair_full, 1)

            def s5_slot(i):
                if i < NST:
                    if i >= 1:
                        pe.wait_ge(bu_free, i)
                    M(PS[:, 4, :], BBT[:, 0, i, :], uT[:, i // 4, 0:T], start=True, stop=True)
                    M(PS[:, 5, :], BBT[:, 1, i, :], uT[:, i // 4, 0:T], start=True, stop=True).then_inc(bu_full, 1)
                if i >= 1:
                    i -= 1
                    q, ii = i // 4, i % 4
                    pe.wait_ge(h_ready, i + 1)
                    if ii == 0 and q:
                        pe.wait_ge(y_free, q)
                    for r in range(2):
                        h = W5[4 + 2 * (i % 2) + r]
                        s, e = ii == 0 and r == 0, ii == 3 and r == 1
                        M(PS[:, 6, :], CCT[:, r, i, :], h[:, 0:T], start=s, stop=e)
                        ins = M(PS[:, 7, 0:NB], CCT[:, r, i, :], h[:, T:NT], start=s, stop=e)
                    ins.then_inc(h_used, 1)
                    if e:
                        pe.wait_ge(h_used, i + 1)
                        pe.sem_inc(y_full, 1)

            for u, unit in enumerate(HEAD_UNITS):
                projection(u, unit)
            pe.wait_ge(pair_free, len(HEAD_UNITS))
            slot = 0
            for i, unit in enumerate(REST_UNITS):
                projection(len(HEAD_UNITS) + i, unit)
                if i % 2 == 1 and slot <= NST:
                    s5_slot(slot)
                    slot += 1
            while slot <= NST:
                s5_slot(slot)
                slot += 1
            pe.wait_ge(pair_free, UA)
            for v in range(8):
                if v >= 2:
                    pe.wait_ge(st_ready, v - 1)
                for i in range(2):
                    for r in range(2):
                        c0 = P * (2 * i + r)
                        ins = tp(PS[0:9, v % 2, c0:c0 + P], hS[:, 2 * v + i, r, :])
                ins.then_inc(st_full, 1)

            pe.wait_ge(w1_in, 16 * 14)
            for k in range(2):
                for s in range(16):
                    f = s // 8
                    ins = M(PS[0:64, 7, k:k + 1], w1c[:, k, s % 8, 64 * (f ^ k):64 * (f ^ k) + 64], peT[:, k, s:s + 1],
                            start=(s == 0), stop=(s == 15))
            ins.then_inc(pos_full, 1)

            def xpose(r):
                b, half, kind, s4 = RS[r]
                n = NCH if b < NB else NCP + 1
                w = r // 4
                if s4 == 0:
                    pe.wait_ge(perm_ready, w + 1)
                    if kind == 1:
                        pe.sem_inc(slab_used, 1)
                if r >= 3:
                    pe.wait_ge(xt_ready, r - 2)
                for g in range(4):
                    ins = tp(PS[:, 4 + r % 3, n * g:n * g + n],
                             ROWSP[0:n, w % 3, g, 2 * s4:2 * s4 + 2, :].rearrange("p s d -> p (s d)"), n)
                ins.then_inc(xt_full, 1)

            def layer1(r):
                b, half, kind, s4 = RS[r]
                n = 4 * (NCH if b < NB else NCP + 1)
                pe.wait_ge(xt_ready, r + 1)
                if b >= 2 and r % 16 == 0:
                    pe.wait_ge(l2_ready, b - 1)
                ins = M(PS[:, 2 * (b % 2) + kind, 0:n], w1c[:, kind, 4 * half + s4, :], XT[:, r % 3, 0:n],
                        start=(half == 0 and s4 == 0), stop=(half == 1 and s4 == 3))
                ins.then_inc(xt_used, 1)
                if r % 16 == 15:
                    pe.wait_ge(xt_used, r + 1)
                    pe.sem_inc(acc_full, 1)

            def layer2(b):
                n = NC if b < NB else NCP
                pe.wait_ge(gelu_ready, b + 1)
                M(PS[0:64, 2 * (b % 2), 0:4 * n], w2[0:64, :], GEL[0:64, 0:4 * n], start=True, stop=True)
                for g in range(4):
                    ins = M(PS[0:n, 2 * (b % 2) + 1, 64 * g:64 * g + 64], GEL[64:128, n * g:n * g + n], w2[64:128, :],
                            start=True, stop=True)
                ins.then_inc(l2_full, 1)

            pe.wait_ge(pos_full, 1)
            for r in range(N_RS + 1):
                if r < N_RS:
                    xpose(r)
                if r >= 1:
                    layer1(r - 1)
                if r >= 16 and r % 16 == 6:
                    layer2(r // 16 - 1)
            layer2(NB)

            pe.wait_ge(qpad_ready, 1)
            pe.wait_ge(l2_ready, NB + 1)
            BP = [(b, p) for b in range(NB) for p in range(2)]
            for c0, w, rhs in ((0, NC, lambda b, p: kcT[:, b, p, 0:NC]),
                               (NC, 1, lambda b, p: kT[:, p, T + b:T + b + 1]),
                               (NC + 1, 1, lambda b, p: kT[:, 2 + p, T + b:T + b + 1])):
                for i, (b, p) in enumerate(BP):
                    M(PS[:, 5, c0:c0 + w], QP[:, p, b, :], rhs(b, p), start=(i == 0), stop=(i == 15))
            M(PS[:, 4, 0:3 * NH], consts[0:NB, CO_BMT:CO_BMT + P], gs8[0:NB, :], start=True,
              stop=True).then_inc(sc_full, 1)

            def key_t(r):
                q, b, p = KR[r]
                n = SLAB[("kpage", (q, b // 4)) if q < 4 else ("winrows", (0, b // 4))]
                if p == 0 and b % 4 == 0:
                    wait_slab(pe, n)
                S = slab(n).rearrange("p (b g c) -> p b g c", b=4, g=4)
                pe.wait_ge(xt_ready, N_RS + max(0, r - 1))
                for g in range(4):
                    ins = tp(PS[:, 6 + r % 2, P * g:P * g + P], S[:, b % 4, g, P * p:P * p + P])
                ins.then_inc(xt_full, 1)
                if p == 1 and b % 4 == 3:
                    pe.wait_ge(xt_full, N_RS + r + 1)
                    pe.sem_inc(slab_used, 1)

            def key_s(r):
                q, b, p = KR[r]
                pe.wait_ge(xt_ready, N_RS + r + 1)
                if r == 64:
                    pe.wait_ge(sc_max, 1)
                ins = M(PS[:, q, :], QP[:, p, b, :], XT[:, (N_RS + r) % 3, :],
                        start=(b == 0 and p == 0), stop=(b == NB - 1 and p == 1))
                ins.then_inc(xt_used, 1)
                if r % 16 == 15:
                    pe.wait_ge(xt_used, N_RS + r + 1)
                    pe.sem_inc(s_full, 1)

            for r in range(len(KR) + 1):
                if r < len(KR):
                    key_t(r)
                if r >= 1:
                    key_s(r - 1)
                if r == 32:
                    pe.wait_ge(pc_ready, 1)
                    M(PS[0:32, 5, 0:NC], consts[:, CO_HSUM:CO_HSUM + 32], SC[:, 0:NC], start=True,
                      stop=True).then_inc(imp_full, 1)
                if r == 56:
                    pe.wait_ge(sel_ready, 1)
                    M(PS[:, 5, 0:NSEL], consts[0:32, CO_HSUMT:CO_HSUMT + P], SSEL, start=True,
                      stop=True).then_inc(selx_full, 1)
            pe.wait_ge(p_ready, 1)
            for v in range(6):
                if v >= 4:
                    pe.wait_ge(pt_ready, v - 3)
                bank = 2 + v % 4
                for g in range(4 if v < 5 else 0):
                    src = SA[:, P * (4 * v + g):P * (4 * v + g) + P] if v < 4 else SW[:, P * g:P * g + P]
                    ins = tp(PS[:, bank, P * g:P * g + P], src)
                if v == 5:
                    tp(PS[0:NC, bank, 0:P], SC[:, 0:NC])
                    tp(PS[0:NB, bank, P:2 * P], PNB[:, 0])
                    ins = tp(PS[0:NB, bank, 2 * P:3 * P], PNB[:, 1])
                ins.then_inc(pt_full, 1)
            pe.wait_ge(pt_ready, 6)
            def out_bank(r, b):
                return PS[0:NH, 4 * r + b // 2, 256 * (b % 2):256 * (b % 2) + 256]

            def new_token(r, b):
                c0 = KVW * (1 + r) + 256
                M(out_bank(r, b), PTN[:, r, NH * b:NH * b + NH], kvs[:, c0:c0 + 256], start=True, stop=False)

            for b in range(NB):
                n = SLAB[("winrows", (1, b // 4))]
                if b % 4 == 0:
                    wait_slab(pe, n)
                S = slab(n).rearrange("p (b g c) -> p b g c", b=4, g=4)
                new_token(1, b)
                for g in range(4):
                    ins = M(out_bank(1, b), PTA[:, 16 + g, NH * b:NH * b + NH], S[:, b % 4, g, :],
                            start=False, stop=(g == 3))
                if b % 4 == 3:
                    ins.then_inc(slab_used, 1)
            for b in range(NB):
                n = SLAB[("vpage", (b,))]
                new_token(0, b)
                M(out_bank(0, b), PTC[0:NC, NH * b:NH * b + NH], vc[0:NC, b, :], start=False, stop=False)
                wait_slab(pe, n)
                S = slab(n).rearrange("p (x c) -> p x c", x=16)
                for x in range(16):
                    ins = M(out_bank(0, b), PTA[:, x, NH * b:NH * b + NH], S[:, x, :], start=False, stop=(x == 15))
                ins.then_inc(slab_used, 1)
            pe.wait_ge(slab_used, SLAB[("vpage", (NB - 1,))] + 1)
            pe.sem_inc(od_full, 1)

            pe.wait_ge(od_ready, 1)
            for t in range(TT):
                for p in range(2):
                    for h in range(HPG):
                        c = 2 * NCP * (HPG * p + h)
                        ins = M(PS[:, t, c:c + 2 * NCP], qT[:, 4 * p + h, P * t:P * t + P],
                                KCZ[:, p].rearrange("p j n -> p (j n)"), start=True, stop=True)
                ins.then_inc(cs_full, 1)
            pe.wait_ge(ot_ready, 1)
            for b in range(NB):
                ins = tp(PS[0:DH, 4, NH * b:NH * b + NH], OS[:, b, :], NH)
            ins.then_inc(ot_full, 1)
            pe.wait_ge(cs_done, 1)
            pe.wait_ge(kz_ready, 2)

            def scores(n):
                t, p, h, j = TASKS[n]
                if n >= 2:
                    pe.wait_ge(as_exp, n - 1)
                for r in range(2):
                    bank = 1 + 2 * (n % 2) + r
                    M(PS[:, bank, 0:P * (t + 1)], qT[:, 4 * p + h, P * t:P * t + P],
                      KZ[:, j, 2 * r + p, 0:P * (t + 1)], start=True, stop=False)
                    ins = M(PS[:, bank, P * t:P * t + P], idb[:, :], maskb[:, :], start=False, stop=True)
                ins.then_inc(as_full, 1)

            def probs(n):
                t, p, h, j = TASKS[n]
                pe.wait_ge(as_p, n + 1)
                if n >= 1:
                    pe.wait_ge(at_a, n)
                    pe.wait_ge(at_d, n)
                for r in range(2):
                    for k in range(t + 1):
                        tp(PS[:, 5 + r, P * k:P * k + P], PP[:, n % 2, r, P * k:P * k + P])
                tp(PS[0:NCP, 0, 0:P], PCP[:, t, (2 * p + j) * HPG + h, :]).then_inc(at_full, 1)

            def values(n):
                t, p, h, j = TASKS[n]
                g = 2 * p + j
                pe.wait_ge(at_a, n + 1)
                pe.wait_ge(at_d, n + 1)
                if n >= 1:
                    pe.wait_ge(ao_free, n)
                for r in range(2):
                    for k in range(t + 1):
                        c0 = 256 * r + 64 * g
                        M(PS[0:64, 7, 0:P], vtm[:, k, c0:c0 + 64], PTP[:, n % 2, 4 * r + k, :],
                          start=(r == 0 and k == 0), stop=False)
                M(PS[0:64, 7, 0:P], vc[0:NCP, NB, 64 * g:64 * g + 64], PTPC[0:NCP, n % 2, :],
                  start=False, stop=True).then_inc(ao_full, 1)

            for n in range(NTK + 2):
                if n < NTK:
                    scores(n)
                if 1 <= n <= NTK:
                    probs(n - 1)
                if n >= 2:
                    values(n - 2)
            pe.wait_ge(ao_free, NTK)

            n = SLAB[("glu", ())]
            wait_slab(pe, n)
            pe.wait_ge(z_ready, 1)
            S = slab(n)[:, 0:2048].rearrange("p (k c) -> p k c", k=4)
            for m in range(4):
                open_pair(U_GLU + m)
                ins = gemm(U_GLU + m, [S[:, k, P * m:P * m + P] for k in range(4)], [zT[:, k, :] for k in range(4)])
                ins.then_inc(pair_full, 1)
            pe.wait_ge(pair_full, U_GLU + 4)
            pe.sem_inc(slab_used, 1)
            for m in range(KD):
                n = SLAB[("mix", (m,))]
                wait_slab(pe, n)
                S = slab(n)[:, 0:3 * D].rearrange("p (w k c) -> p w k c", w=3, c=P)
                S5 = slab(n)[:, 3 * D:3 * D + 512].rearrange("p (k c) -> p k c", c=P)
                for w in range(4):
                    u = U_MIX + 4 * m + w
                    open_pair(u)
                    if m == 0 and w == 3:
                        pe.wait_ge(os5_ready, 4)
                    src = (hT, hT, oT, uT)[w]
                    nk = KD if w < 3 else 4
                    ins = gemm(u, [(S[:, w, k, :] if w < 3 else S5[:, k, :]) for k in range(nk)],
                               [src[:, k, :] for k in range(nk)])
                    ins.then_inc(pair_full, 1)
                pe.wait_ge(pair_full, U_MIX + 4 * m + 4)
                pe.sem_inc(slab_used, 1)

            def out_units(base, key, kt, per, src, stage):
                for i, (kind, m) in enumerate(OUT_ORDER):
                    u = base + i
                    open_pair(u)
                    if kind == "g":
                        n = SLAB[(key, (m // per,))]
                        wait_slab(pe, n)
                        S = slab(n).rearrange("p (k c) -> p k c", k=kt)
                        c = P * (m % per)
                        ins = gemm(u, [S[:, k, c:c + P] for k in range(kt)], [src[:, k, :] for k in range(kt)])
                        ins.then_inc(pair_full, 1)
                        if m % per == per - 1:
                            pe.wait_ge(pair_full, u + 1)
                            pe.sem_inc(slab_used, 1)
                    else:
                        back(u, stage[:, m % 2, :]).then_inc(pair_full, 1)

            pe.wait_ge(mix_ready, KD)
            out_units(U_OUT, "out", KD, 4, mT, zo)
            norm_transposes(10, xn2)
            pe.wait_ge(xnt_free, 20)
            for m in range(KF):
                u = U_UP + m
                open_pair(u)
                n = SLAB[("up", (m // 4,))]
                wait_slab(pe, n)
                S = slab(n).rearrange("p (k c) -> p k c", k=KD)
                c = P * (m % 4)
                ins = gemm(u, [S[:, k, c:c + P] for k in range(KD)], [hT[:, k, :] for k in range(KD)])
                ins.then_inc(pair_full, 1)
                if m % 4 == 3:
                    pe.wait_ge(pair_full, u + 1)
                    pe.sem_inc(slab_used, 1)
            pe.wait_ge(f_ready, KF)
            out_units(U_DOWN, "down", KF, 1, fT, hT)


INPUTS = ["x_prompt", "x_sample", "cache_kv_cmp", "cache_kv_slc", "state_kv_win", "state_s5", "page_table",
          "norm_mix_pre", "norm_mix_post", "norm_mlp_pre", "norm_mlp_post", "w_in",
          "cmp_pe_k", "cmp_w1_k", "cmp_w2_k", "cmp_pe_v", "cmp_w1_v", "cmp_w2_v",
          "s5_a_re", "s5_a_im", "s5_log_dt", "s5_b_re", "s5_b_im", "s5_c_re", "s5_c_im", "s5_d", "s5_w_glu",
          "s5_b_glu", "w_branch_nsa", "w_branch_s5", "w_out", "w_mlp_up", "w_mlp_down"]
KVS = (2, NG, DH)
OUTPUTS = [("y_prompt", (1, T, D)), ("y_sample", (NB, 1, D)),
           ("kv_cmp_prompt", (1, T) + KVS), ("kv_slc_prompt", (1, T) + KVS), ("kv_win_prompt", (1, WIN) + KVS),
           ("s5_prompt", (1, G5, N5, 2)),
           ("kv_cmp_sample", (NB, 1) + KVS), ("kv_slc_sample", (NB, 1) + KVS), ("kv_win_sample", (NB, WIN) + KVS),
           ("s5_sample", (NB, G5, N5, 2))]


def kernel(**inputs):
    import concourse.bacc as bacc
    from concourse.bass_utils import run_bass_kernel_spmd

    nc = bacc.Bacc("TRN2", target_bir_lowering=False, num_devices=1)
    consts, tie = shape_constants()
    arrays, aps = {}, {}
    given = {name: np.ascontiguousarray(inputs[name]) for name in INPUTS}
    given["consts"], given["tie"] = consts, tie
    for name, v in given.items():
        arrays[f"in_{name}"] = v
        aps[name] = nc.dram_tensor(f"in_{name}", v.shape, mybir.dt.from_np(v.dtype), kind="ExternalInput").ap()
    for name, shape in OUTPUTS:
        aps[name] = nc.dram_tensor(f"out_{name}", shape, F32, kind="ExternalOutput").ap()
    build(nc, aps)
    r = run_bass_kernel_spmd(nc, [arrays], core_ids=[0])
    return tuple(r.results[0][f"out_{name}"] for name, _ in OUTPUTS)
```

```python
from contextlib import ExitStack

import numpy as np
import concourse.bass as bass
from concourse import mybir

ALU = mybir.AluOpType
ACT = mybir.ActivationFunctionType
AX = mybir.AxisListType.X
F32 = mybir.dt.float32
BF16 = mybir.dt.bfloat16
I32 = mybir.dt.int32

P = 128
D = 1024
KD = D // P
T = 512
TT = T // P
NB = 8
NT = T + NB
HALF = NT // 2
PAGE = 128
N_PAGES = 16
N_PHYS = 160
NG, HPG, DH = 4, 4, 64
NH = NG * HPG
KVW = 2 * NG * DH
STRIDE = 16
NCH = N_PAGES * PAGE // STRIDE
NC = NCH - 1
NCP = T // STRIDE - 1
SELB = 64
NSEL = 33
TOPK = 16
WIN = 512
G5, N5, C5 = 32, 64, 16
NST = G5 // 2
FF = 4096
KF = FF // P
EPS = 1e-6
NEG = -1e30
FORCE = 1e4
C_KV = 1024
C_GN = C_KV + 3 * KVW
C_U = C_GN + 3 * NH
C_GM = C_U + 512
TWO_PI = 2.0 * np.pi
RND = 12582912.0

SLOT = 4096
NS = 3

CO_ID = 0
CO_MASK = CO_ID + P
CO_CMASK = CO_MASK + P
CO_ROWV = CO_CMASK + TT * NCP
CO_HSUM = CO_ROWV + TT
CO_HSUMT = CO_HSUM + 32
CO_BM = CO_HSUMT + P
CO_BMT = CO_BM + NB
CO_HM = CO_BMT + P
CO_ROW = CO_HM + NH
CO_GM16 = CO_ROW + 2
CO_N = CO_GM16 + 4 * NB


def shape_constants():
    c = np.zeros((P, CO_N), np.float32)
    i = np.arange(P)
    c[:, CO_ID:CO_ID + P] = np.eye(P)
    c[:, CO_MASK:CO_MASK + P] = np.where(i[None, :] > i[:, None], NEG, 0)
    for t in range(TT):
        q = i + P * t
        ok = (16 * np.arange(NCP) + 31)[None, :] <= q[:, None]
        c[:, CO_CMASK + NCP * t:CO_CMASK + NCP * (t + 1)] = np.where(ok, 0, NEG)
        c[:, CO_ROWV + t] = q >= 31
    c[:, CO_HSUM:CO_HSUM + 32] = i[:, None] // HPG == np.arange(32)[None, :]
    c[:32, CO_HSUMT:CO_HSUMT + P] = i[None, :] // HPG == np.arange(32)[:, None]
    c[:, CO_BM:CO_BM + NB] = i[:, None] // NH == np.arange(NB)[None, :]
    c[:NB, CO_BMT:CO_BMT + P] = i[None, :] // NH == np.arange(NB)[:, None]
    c[:, CO_HM:CO_HM + NH] = i[:, None] % NH == np.arange(NH)[None, :]
    c[:, CO_ROW], c[:, CO_ROW + 1] = 2 * i, 2 * (i % 8)
    c[:, CO_GM16:CO_GM16 + 4 * NB] = (np.arange(4 * NB) % NG)[None, :] == (i // HPG)[:, None]
    j = np.arange(NSEL)
    tie = np.broadcast_to((j[None, :] < j[:, None]).astype(np.float32), (32, NSEL, NSEL)).copy()
    return c, tie


def stream_plan():
    plan = [("win", (C_U, 512), 1, 0)]
    plan += [("win", (C_KV + KVW * c, 512), 1, 0) for c in range(3)]
    plan += [("win", (C_GN, 3 * NH), 1, 0)]
    plan += [("q", (p,), 8, 0) for p in (1, 0)]
    for b in range(NB):
        plan += [("cmp", (b, half), 0, 1) for half in range(2)]
    plan += [("cmp", (NB, half), 1, 0) for half in range(2)]
    for q in range(4):
        plan += [("kpage", (q, bh), 8, 8) for bh in range(2)]
    plan += [("winrows", (0, bh), 4, 0) for bh in range(2)]
    plan += [("winrows", (1, bh), 4, 0) for bh in range(2)]
    plan += [("vpage", (b,), 8, 8) for b in range(NB)]
    plan += [("glu", (), 1, 0)]
    plan += [("mix", (m,), 7, 0) for m in range(KD)]
    plan += [("out", (m,), 1, 0) for m in range(2)]
    plan += [("up", (m,), 1, 0) for m in range(KF // 4)]
    plan += [("down", (m,), 1, 0) for m in range(KD)]
    return plan


PLAN = stream_plan()
SLAB = {(k, a): n for n, (k, a, _, _) in enumerate(PLAN)}


def landed_counts(who):
    counts, total = [], [0] * NS
    for n, entry in enumerate(PLAN):
        total[n % NS] += 16 * entry[2 + who]
        counts.append(total[n % NS])
    return counts


LANDED = [landed_counts(0), landed_counts(1)]


def projection_units():
    u_tiles = [("gemm", ("win", (C_U, 512)), m, P, ("u", m)) for m in range(4)]
    units = u_tiles[:3] + [("bb", ri, q) for ri in range(2) for q in range(4)] + u_tiles[3:]
    units += [("cc", ri, q) for ri in range(2) for q in range(4)]
    units += [("h0",), ("bus",)]
    rest = []
    prev = None
    for c in range(3):
        for m in range(4):
            rest.append(("gemm", ("win", (C_KV + KVW * c, 512)), m, P, ("kv", c, m)))
            if prev is not None:
                rest.append(("tr", *prev))
            prev = (c, m)
    rest.append(("tr", *prev))
    rest.append(("gemm", ("win", (C_GN, 3 * NH)), 0, 3 * NH, ("gn",)))
    q_units = [("gemm", ("q", (i // 4,)), i % 4, P, ("q", i)) for i in (6, 7, 4, 5, 0, 1, 2, 3)]
    rest += q_units[:1] + [("trg",)] + q_units[1:]
    return units, rest


HEAD_UNITS, REST_UNITS = projection_units()
N_UNITS_A = len(HEAD_UNITS) + len(REST_UNITS)
KV_TILES = [(c, m) for c in range(3) for m in range(4)]


def build(nc, a):
    with ExitStack() as ctx:
        def sb(name, shape, dt=F32):
            return ctx.enter_context(nc.sbuf_tensor(name, shape, dt))

        def sem(name):
            return ctx.enter_context(nc.semaphore(name))

        consts = sb("consts", [P, CO_N])
        idb = sb("idb", [P, P], BF16)
        maskb = sb("maskb", [P, P], BF16)
        pages = sb("pages", [P, NB * N_PAGES], I32)
        pages8 = sb("pages8", [P, NB], I32)
        row_kv = sb("row_kv", [P, 2, NB * N_PAGES], I32)
        row_cmp = sb("row_cmp", [P, 2, NB], I32)
        hT = sb("hT", [P, KD, NT])
        QO = sb("QO", [P, 2 * KD * NT])
        KVU = sb("KVU", [P, 12 * NT])
        kvs = sb("kvs", [NB, 3 * KVW])
        R = sb("R", [P, 16896])
        stream = sb("stream", [P, NS, SLOT])
        small = sb("small", [P, 1600])

        qT = QO[:, 0:KD * NT].rearrange("p (k t) -> p k t", t=NT)
        oT = QO[:, KD * NT:].rearrange("p (k t) -> p k t", t=NT)
        kT = KVU[:, 0:4 * NT].rearrange("p (k t) -> p k t", t=NT)
        vtm = KVU[:, 4 * NT:4 * NT + 2048].rearrange("p (t c) -> p t c", t=TT)
        uT = KVU[:, 8 * NT:12 * NT].rearrange("p (k t) -> p k t", t=NT)

        ident = consts[:, CO_ID:CO_ID + P]
        used = [0]

        def tiny(n):
            used[0] += n
            assert used[0] <= 1600
            return small[:, used[0] - n:used[0]]

        gT = tiny(2 * KD).rearrange("p (w k) -> p w k", w=2)
        are, aim, ldt = tiny(NST), tiny(NST), tiny(NST)
        dt, mag, ang, ang2, sn, sh, cs = (tiny(NST) for _ in range(7))
        abr, abi, nabi, den, cor, coi, s5t, s5u = (tiny(NST) for _ in range(8))
        ur, ui, tp0, tp1 = (tiny(NST) for _ in range(4))
        ssq, rstd = tiny(5), tiny(5)
        epsb = tiny(1)
        sqm = tiny(5 * KD).rearrange("p (t m) -> p t m", t=5)
        s5d, bglu = tiny(4), tiny(4)
        h0T = tiny(2 * NST * NB).rearrange("p (i r b) -> p i r b", i=NST, r=2)
        buS = tiny(2 * NST * NB).rearrange("p (i r b) -> p i r b", i=NST, r=2)
        hS = tiny(2 * NST * 9).rearrange("p (i r b) -> p i r b", i=NST, r=2)
        sst = tiny(4 * NB).rearrange("p (k b) -> p k b", k=4)
        gtm = tiny(TT * 3 * NH).rearrange("p (t c) -> p t c", t=TT)
        gs8 = tiny(3 * NH)
        gsTs = tiny(NB)
        pos = tiny(1)
        gd = tiny(3)
        dmx, dsm, dinv = tiny(3), tiny(3), tiny(3)
        amx, asm, ainv = tiny(8), tiny(8), tiny(8)
        cmx, csm = tiny(NH), tiny(NH)
        pmx = tiny(4)

        PS = ctx.enter_context(nc.psum_tensor("PS", [P, 8, 512], F32))

        consts_in = sem("consts_in")
        x_in = [sem(f"x_in_{t}") for t in range(TT + 1)]
        g_in = sem("g_in")
        pages_in = sem("pages_in")
        rows_ready = sem("rows_ready")
        perm_ready = sem("perm_ready")
        par_in = sem("par_in")
        slab_in = [sem(f"slab_in{i}") for i in range(NS)]
        rows_in = [sem(f"rows_in{i}") for i in range(NS)]
        slab_used = sem("slab_used")
        act_ch = sem("act_ch")
        dve_ch = sem("dve_ch")
        pool_ch = sem("pool_ch")
        masks_ready = sem("masks_ready")
        zero_ready = sem("zero_ready")
        yg_ready = sem("yg_ready")
        ssq_ready = sem("ssq_ready")
        root_ready = sem("root_ready")
        xn_ready = sem("xn_ready")
        xnt_full = sem("xnt_full")
        xnt_free = sem("xnt_free")
        pair_full = sem("pair_full")
        pair_free = sem("pair_free")
        ldt_ready = sem("ldt_ready")
        ang_ready = sem("ang_ready")
        trig_ready = sem("trig_ready")
        unit_ready = sem("unit_ready")
        bb_ready = sem("bb_ready")
        c_in = sem("c_in")
        h0_in = sem("h0_in")
        table_ready = sem("table_ready")
        bu_full = sem("bu_full")
        bu_free = sem("bu_free")
        h_ready = sem("h_ready")
        h_used = sem("h_used")
        y_full = sem("y_full")
        y_free = sem("y_free")
        st_full = sem("st_full")
        st_ready = sem("st_ready")
        kv_store = [sem(f"kv_store{i}") for i in range(4)]
        stores = sem("stores")
        copies = sem("copies")
        w1_in = sem("w1_in")
        pos_full = sem("pos_full")
        xt_full = sem("xt_full")
        xt_ready = sem("xt_ready")
        xt_used = sem("xt_used")
        acc_full = sem("acc_full")
        pre_ready = sem("pre_ready")
        gelu_ready = sem("gelu_ready")
        l2_full = sem("l2_full")
        l2_ready = sem("l2_ready")
        qpad_ready = sem("qpad_ready")
        sc_full = sem("sc_full")
        sc_max = sem("sc_max")
        sc_exp = sem("sc_exp")
        pc_ready = sem("pc_ready")
        imp_full = sem("imp_full")
        sel_ready = sem("sel_ready")
        selx_full = sem("selx_full")
        s_full = sem("s_full")
        smax = sem("smax")
        sexp = sem("sexp")
        p_ready = sem("p_ready")
        pt_full = sem("pt_full")
        pt_ready = sem("pt_ready")
        od_full = sem("od_full")
        cs_full = sem("cs_full")
        cs_max = sem("cs_max")
        cs_exp = sem("cs_exp")
        ot_done = sem("ot_done")
        as_full = sem("as_full")
        as_max = sem("as_max")
        as_exp = sem("as_exp")
        as_rec = sem("as_rec")
        as_p = sem("as_p")
        as_pw = sem("as_pw")
        at_full = sem("at_full")
        at_a = sem("at_a")
        at_d = sem("at_d")
        ao_full = sem("ao_full")
        ao_free = sem("ao_free")
        z_ready = sem("z_ready")
        os5_ready = sem("os5_ready")
        mix_ready = sem("mix_ready")
        gain_in = sem("gain_in")
        x2_in = sem("x2_in")
        x1_ready = sem("x1_ready")
        f_ready = sem("f_ready")
        tie_in = sem("tie_in")
        od_ready = sem("od_ready")
        kz_ready = sem("kz_ready")
        selx_read = sem("selx_read")
        samax = sem("samax")
        saexp = sem("saexp")
        pa_ready = sem("pa_ready")
        oe_full = sem("oe_full")
        ot_ready = sem("ot_ready")
        ot_full = sem("ot_full")
        s5_store = sem("s5_store")

        BBT = R[:, 0:4096].rearrange("p (r i c) -> p r i c", r=2, i=NST)
        CCT = R[:, 4096:8192].rearrange("p (r i c) -> p r i c", r=2, i=NST)
        BBP = R[:, 8192:12288].rearrange("p (r i c) -> p r i c", r=2, i=NST)
        CCP = R[:, 12288:16384].rearrange("p (r i c) -> p r i c", r=2, i=NST)
        TAB = R[:, 8192:16384].rearrange("p (s r i t) -> p s r i t", s=2, r=2, i=4)
        WK = R[:, 16384:16896]
        STO = QO[0:9, KD * NT:KD * NT + 4096].rearrange("p (i c r) -> p i c r", i=NST, r=2)
        bld = R[:, 0:512].rearrange("p (r i c) -> p r i c", r=2, i=NST)
        bwk = R[:, 512:1536].rearrange("p (r i c) -> p r i c", r=4, i=NST)
        xtm = KVU[:, 0:5 * D].rearrange("p (t d) -> p t d", d=D)
        xn = QO[:, 0:2 * D].rearrange("p (s d) -> p s d", s=2)
        junk = QO[:, 2 * D:3 * D]
        st0 = QO[0:NB, KD * NT:KD * NT + 4096].rearrange("b (i c r) -> b i r c", i=NST, r=2)
        W5 = [QO[:, KD * NT + NT * i:KD * NT + NT * (i + 1)] for i in range(8)]
        zst = QO[:, 2048:2048 + 2 * NT].rearrange("p (s t) -> p s t", s=2)
        kst = QO[:, 0:2048].rearrange("p (s t c) -> p s t c", s=4, t=TT)
        gsT = zst[0:3 * NH, 0, 0:T]

        XT = R[:, 0:1536].rearrange("p (s c) -> p s c", s=3)
        w1c = R[:, 1536:3584].rearrange("p (k s h) -> p k s h", k=2, s=8)
        w2 = R[:, 3584:3648]
        SH = R[:, 3680:4192]
        PRE = R[:, 4192:4704]
        GEL = R[:, 4704:5216]
        peT = R[:, 3648:3680].rearrange("p (k s) -> p k s", k=2)
        kcT = R[:, 5216:5216 + 8 * 2 * (NC + 2)].rearrange("p (b q n) -> p b q n", b=8, q=2)
        vc = R[:, 7520:9824].rearrange("p (b c) -> p b c", b=9)
        ROWSP = R[:, 9824:9824 + 6144].rearrange("p (w g s d) -> p w g s d", w=3, g=4, s=8)
        QP = R[:, 9824:11872].rearrange("p (q b c) -> p q b c", q=2, b=NB)
        SA = R[:, 11872:13921]
        SW = R[:, 13921:14434]
        SC = R[:, 14434:14563]
        IMP = R[0:32, 14564:14697]
        SSEL = R[0:32, 14700:14733]
        SELX = R[:, 14740:14773]
        GH = R[:, 14780:14828]
        CMPA = R[0:32, 14828:15917].rearrange("p (j i) -> p j i", j=NSEL)
        CMPB = R[0:32, 1536:2625].rearrange("p (j i) -> p j i", j=NSEL)
        TIE = R[0:32, 2625:3714].rearrange("p (j i) -> p j i", j=NSEL)
        PTA = R[:, 1536:4096].rearrange("p (g c) -> p g c", c=P)
        PTN = R[0:NB, 4096:4352].rearrange("p (r c) -> p r c", r=2)
        PTC = R[:, 4352:4480]
        PNB = R[:, 4480:4496].rearrange("p (r b) -> p r b", r=2)
        OD = R[0:NH, 9824:11872].rearrange("p (x d) -> p x d", d=DH)
        OE = R[0:NH, 11872:13920].rearrange("p (x d) -> p x d", d=DH)
        OS = R[0:NH, 16160:16672].rearrange("p (b d) -> p b d", d=DH)
        KCZ = R[:, 16672:16796].rearrange("p (q j n) -> p q j n", q=2, j=2)
        KZ = R[:, 0:4096].rearrange("p (j k t) -> p j k t", j=2, k=4)
        PP = R[:, 9824:11872].rearrange("p (s r c) -> p s r c", s=2, r=2)
        PTP = R[:, 11872:13920].rearrange("p (s k c) -> p s k c", s=2, k=2)
        PTPC = R[:, 14176:14688].rearrange("p (s c) -> p s c", s=2)
        PCP = R[:, 5216:5216 + TT * NH * NCP].rearrange("p (t h n) -> p t h n", t=TT, h=NH)
        zT = R[:, 0:4 * NT].rearrange("p (k t) -> p k t", t=NT)
        sgl = R[:, 4 * NT:6 * NT].rearrange("p (s t) -> p s t", s=2)
        mxb = R[:, 6 * NT:14 * NT].rearrange("p (s k t) -> p s k t", s=2, k=4)
        mT = R[:, 14 * NT:22 * NT].rearrange("p (k t) -> p k t", t=NT)
        zo = R[:, 22 * NT:24 * NT].rearrange("p (s t) -> p s t", s=2)
        ytm = KVU[:, 0:5 * D].rearrange("p (t d) -> p t d", d=D)
        x1 = QO[:, 0:5 * D].rearrange("p (t d) -> p t d", d=D)
        xn2 = QO[:, 5 * D:7 * D].rearrange("p (s d) -> p s d", s=2)
        gain = QO[:, 7 * D:8 * D]
        sqj = KVU[:, 5 * D:5 * D + 5 * P].rearrange("p (t c) -> p t c", t=5)
        fT = R[:, 0:KF * NT].rearrange("p (k t) -> p k t", t=NT)

        def slab(n):
            return stream[:, n % NS, :]

        def slab_page(kind, arg, x):
            if kind == "kpage":
                return (4 * arg[1] + x // 4) * N_PAGES + 4 * arg[0] + x % 4
            return arg[0] * N_PAGES + x

        def wait_slab(eng, n):
            if PLAN[n][2]:
                eng.wait_ge(slab_in[n % NS], LANDED[0][n])
            if PLAN[n][3]:
                eng.wait_ge(rows_in[n % NS], LANDED[1][n])

        def pair(u):
            return PS[:, 2 * (u % 2):2 * (u % 2) + 2, :]

        def halves(ap):
            return ap.rearrange("p (h t) -> p h t", h=2)

        UA = N_UNITS_A
        U_GLU = UA
        U_MIX = U_GLU + 4
        U_OUT = U_MIX + 4 * KD
        U_UP = U_OUT + 2 * KD
        U_DOWN = U_UP + KF
        RS = [(b, half, kind, s4) for b in range(NB + 1) for half in range(2) for kind in range(2) for s4 in range(4)]
        KR = [(q, b, p) for q in range(5) for b in range(NB) for p in range(2)]
        N_RS = len(RS)
        TASKS = [(t, p, h, j, 2 if t < 2 else 1) for t in range(TT) for p in range(2)
                 for h in range(0, HPG, 2 if t < 2 else 1) for j in range(2)]
        NTK = len(TASKS)
        R_IMP, R_SEL, R_SA = 24, 40, 70
        R_CS = [44 + 8 * t for t in range(TT)]
        R_CE = [r + (4 if t < TT - 1 else 6) for t, r in enumerate(R_CS)]
        PT_BANK = (0, 1, 2, 3, 6, 7)

        def softmaxes(n):
            if TASKS[n][4] == 1:
                return [(r, 0, r, r, 0) for r in range(2)]
            return [(2 * x + r, x, r, x, 256 * r) for x in range(2) for r in range(2)]

        def scale_probs(eng, n, i, x, r, bank, c0):
            t, p, h, j, nx = TASKS[n]
            col = 3 * ((2 * p + j) * HPG + h + x) + 1 + r
            k = 4 * (n % 2) + i
            S = PP[:, n % 2, bank, c0:c0 + P * (t + 1)]
            return eng.tensor_scalar(S, S, ainv[:, k:k + 1], gtm[:, t, col:col + 1], ALU.mult, ALU.mult)

        def blocks(n, ap, w):
            if TASKS[n][4] == 1:
                return ap[:, 0:w].unsqueeze(1)
            return ap.rearrange("p (r c) -> p r c", r=2)[:, :, 0:w]
        OUT_ORDER = [("g", 0)]
        for m_ in range(1, KD):
            OUT_ORDER += [("g", m_), ("t", m_ - 1)]
        OUT_ORDER.append(("t", KD - 1))

        block = ctx.enter_context(nc.Block())

        @block.sync
        def _(sp):
            sp.dma_start(consts[:, :], a["consts"]).then_inc(consts_in, 16)
            def par(dst, src):
                sp.dma_start(dst, src, allow_slow_non_contiguous=True).then_inc(par_in, 16)

            for t in range(TT):
                sp.dma_start(xtm[:, t, :], a["x_prompt"][0, P * t:P * t + P, :]).then_inc(x_in[t], 16)
            sp.dma_start(xtm[0:NB, TT, :], a["x_sample"].rearrange("b o d -> (b o) d")).then_inc(x_in[TT], 16)
            for w, name in enumerate(("norm_mix_pre", "norm_mlp_pre")):
                sp.dma_start(gT[:, w, :], a[name].rearrange("(k p) -> p k", p=P),
                             allow_slow_non_contiguous=True).then_inc(g_in, 16)

            def small_loads():
                for dst, name in ((are, "s5_a_re"), (aim, "s5_a_im")):
                    for g in range(2):
                        par(dst[64 * g:64 * g + 64, :], a[name].rearrange("(i g) n -> g n i", g=2)[g])
                for g in range(2):
                    par(ldt[64 * g:64 * g + 64, :],
                        a["s5_log_dt"].rearrange("(o i g) -> g o i", g=2, o=1)[g].to_broadcast([64, NST]))
                for r, name in enumerate(("s5_b_re", "s5_b_im")):
                    for g in range(2):
                        par(bld[64 * g:64 * g + 64, r, :, :], a[name].rearrange("(i g) n c -> g n i c", g=2)[g])
                par(s5d[:, :], a["s5_d"].rearrange("(k p) -> p k", p=P))
                par(bglu[:, :], a["s5_b_glu"].rearrange("(k p) -> p k", p=P))
                sp.dma_start(QO[0:NB, KD * NT:KD * NT + 4096],
                              a["state_s5"].rearrange("b g n r -> b (g n r)")).then_inc(h0_in, 16)

                sp.dma_start(pages[:, :], a["page_table"].rearrange("b (o n) -> o (b n)", o=1).to_broadcast(
                    [P, NB * N_PAGES])).then_inc(pages_in, 16)
                for g in range(N_PAGES):
                    sp.dma_start(pages8[8 * g:8 * g + 8, :], a["page_table"].rearrange("b (o n) -> n o b", o=1)[g]
                                  .to_broadcast([8, NB]), allow_slow_non_contiguous=True).then_inc(pages_in, 16)

            wq = a["w_in"].rearrange("(k p) c -> p k c", p=P)
            slc = a["cache_kv_slc"].rearrange("n t k g d -> n t (k g d)")
            def compression_weights():
                sp.wait_ge(bu_full, NST)
                for k, kv in enumerate("kv"):
                    w1 = a[f"cmp_w1_{kv}"].rearrange("(f s e) d h -> f e d s h", f=2, e=2)
                    for f in range(2):
                        col = 64 * (f ^ k)
                        for e in range(2):
                            sp.dma_start(w1c[64 * e:64 * e + 64, k, :, col:col + 64], w1[f, e]).then_inc(w1_in, 16)
                    sp.dma_start(w2[64 * k:64 * k + 64, :], a[f"cmp_w2_{kv}"]).then_inc(w1_in, 16)
                    for e in range(2):
                        sp.dma_start(peT[64 * e:64 * e + 64, k, :],
                                      a[f"cmp_pe_{kv}"].rearrange("(s e) d -> e d s", e=2)[e],
                                      allow_slow_non_contiguous=True).then_inc(w1_in, 16)

            for n, (kind, arg, count, _) in enumerate(PLAN):
                if (kind, arg) == ("cmp", (0, 0)):
                    compression_weights()
                if count == 0:
                    continue
                if n >= NS:
                    sp.wait_ge(slab_used, n - NS + 1)
                S = slab(n)
                done = slab_in[n % NS]
                if kind == "win":
                    c0, w = arg
                    sp.dma_start(S[:, 0:KD * w].rearrange("p (k c) -> p k c", c=w),
                                 wq[:, :, c0:c0 + w]).then_inc(done, 16)
                    if n == 0:
                        small_loads()
                elif kind == "q":
                    dst = S.rearrange("p (k h j d) -> p k h j d", k=KD, h=HPG, j=2)
                    for j in range(2):
                        for h in range(HPG):
                            c0 = ((2 * arg[0] + j) * HPG + h) * DH
                            sp.dma_start(dst[:, :, h, j, :], wq[:, :, c0:c0 + DH]).then_inc(done, 16)
                elif kind == "cmp":
                    for s_ in kv_store:
                        sp.wait_ge(s_, 16 * len(KV_TILES) // 4)
                    sp.dma_start(S[0:NCP + 1, :], a["kv_cmp_prompt"].rearrange(
                        "o (n f s) k g d -> f (o n) (s k g d)", f=2, s=8)[arg[1]]).then_inc(done, 16)
                elif kind == "winrows":
                    kv, bh = arg
                    dst = S.rearrange("p (b g c) -> p b g c", b=4, g=4)
                    for b4 in range(4):
                        src = a["state_kv_win"][4 * bh + b4].rearrange("(g t) k x d -> t k g (x d)", t=P)[:, kv]
                        sp.dma_start(dst[:, b4], src).then_inc(done, 16)
                elif kind in ("kpage", "vpage"):
                    sp.wait_ge(pages_in, 16 * (1 + N_PAGES))
                    kv = int(kind == "vpage")
                    dst = S.rearrange("p (x c) -> p x c", x=16)
                    for x in range(0, 16, 2):
                        at = slab_page(kind, arg, x)
                        v = sp.value_load(pages[0:1, at:at + 1], min_val=0, max_val=N_PHYS - 1)
                        sp.dma_start(dst[:, x, :], slc[bass.DynSlice(v, 1)].rearrange("o t c -> (o t) c")
                                     [:, 256 * kv:256 * kv + 256]).then_inc(done, 16)
                elif kind == "glu":
                    sp.dma_start(S[:, 0:2048].rearrange("p (k c) -> p k c", k=4),
                                 a["s5_w_glu"].rearrange("(k p) c -> p k c", p=P)).then_inc(done, 16)
                elif kind == "mix":
                    c0 = arg[0] * P
                    dst = S[:, 0:3 * D].rearrange("p (w k c) -> p w k c", w=3, c=P)
                    for w in range(2):
                        sp.dma_start(dst[:, w], wq[:, :, C_GM + w * D + c0:C_GM + w * D + c0 + P]).then_inc(done, 16)
                    wn = a["w_branch_nsa"].rearrange("(q j h d) c -> q j d h c", q=2, j=2, h=HPG)
                    for q in range(2):
                        for j in range(2):
                            sp.dma_start(dst[64 * j:64 * j + 64, 2, 4 * q:4 * q + 4, :],
                                         wn[q, j][:, :, c0:c0 + P]).then_inc(done, 16)
                    sp.dma_start(S[:, 3 * D:3 * D + 512].rearrange("p (k c) -> p k c", c=P),
                                 a["w_branch_s5"].rearrange("(k p) c -> p k c", p=P)[:, :, c0:c0 + P]
                                 ).then_inc(done, 16)
                elif kind == "out":
                    sp.dma_start(S.rearrange("p (k c) -> p k c", c=512),
                                 a["w_out"].rearrange("(k p) c -> p k c", p=P)[:, :, 512 * arg[0]:512 * arg[0] + 512]
                                 ).then_inc(done, 16)
                elif kind == "up":
                    sp.dma_start(S.rearrange("p (k c) -> p k c", c=512),
                                 a["w_mlp_up"].rearrange("(k p) c -> p k c", p=P)[:, :, 512 * arg[0]:512 * arg[0] + 512]
                                 ).then_inc(done, 16)
                elif kind == "down":
                    sp.dma_start(S.rearrange("p (k c) -> p k c", c=P),
                                 a["w_mlp_down"].rearrange("(k p) c -> p k c", p=P)[:, :, P * arg[0]:P * arg[0] + P]
                                 ).then_inc(done, 16)

        ROWS = [P] * TT + [NB]
        N_PAR = 12
        NORM_UNITS = [(t, half) for t in range(5) for half in range(2)]

        @block.gpsimd
        def _(pool):
            n_ch = [0]

            def link(ins):
                n_ch[0] += 1
                ins.then_inc(pool_ch, 1)
                pool.wait_ge(pool_ch, n_ch[0])

            nc.gpsimd.memset(R[:, 8192:12288], 0.0).then_inc(zero_ready, 1)
            nc.gpsimd.memset(R[:, 12288:16384], 0.0).then_inc(zero_ready, 1)
            pool.wait_ge(unit_ready, 1)
            for grp in range(4):
                if grp < 2:
                    pool.wait_ge(pair_free, HEAD_UNITS.index(("bb", 1, 3) if grp == 0 else ("cc", 1, 3)) + 1)
                if grp >= 2:
                    pool.wait_ge(h_ready, 4 * (grp - 1))
                tr, ti = TAB[:, grp % 2, 0], TAB[:, grp % 2, 1]
                c = slice(4 * grp, 4 * grp + 4)
                nc.gpsimd.memset(tr[:, :, 0:1], 1.0)
                nc.gpsimd.memset(ti[:, :, 0:1], 0.0)
                nc.gpsimd.tensor_copy(ur[:, c], cs[:, c])
                link(nc.gpsimd.tensor_copy(ui[:, c], sn[:, c]))
                m = 1
                while m < T:
                    w = min(m, P)
                    for o in range(0, m, w):
                        Ur, Ui = (x[:, c].unsqueeze(2).to_broadcast([P, 4, w]) for x in (ur, ui))
                        Ar, Ai = (x[:, :, o:o + w] for x in (tr, ti))
                        Br, Bi = (x[:, :, m + o:m + o + w] for x in (tr, ti))
                        wk = WK[:, 0:4 * w].rearrange("p (i t) -> p i t", i=4)
                        nc.gpsimd.tensor_tensor(Br, Ar, Ur, ALU.mult)
                        link(nc.gpsimd.tensor_tensor(wk, Ai, Ui, ALU.mult))
                        link(nc.gpsimd.tensor_tensor(Br, Br, wk, ALU.subtract))
                        nc.gpsimd.tensor_tensor(Bi, Ar, Ui, ALU.mult)
                        link(nc.gpsimd.tensor_tensor(wk, Ai, Ur, ALU.mult))
                        link(nc.gpsimd.tensor_tensor(Bi, Bi, wk, ALU.add))
                    m *= 2
                    if m < T:
                        nc.gpsimd.tensor_tensor(tp0[:, c], ui[:, c], ui[:, c], ALU.mult)
                        link(nc.gpsimd.tensor_tensor(tp1[:, c], ur[:, c], ui[:, c], ALU.mult))
                        link(nc.gpsimd.tensor_tensor(ur[:, c], ur[:, c], ur[:, c], ALU.mult))
                        link(nc.gpsimd.tensor_tensor(ur[:, c], ur[:, c], tp0[:, c], ALU.subtract))
                        link(nc.gpsimd.tensor_tensor(ui[:, c], tp1[:, c], tp1[:, c], ALU.add))
                nc.gpsimd.tensor_copy(tp0[:, 0:1], ur[:, 0:1]).then_inc(table_ready, 1)
            pool.wait_ge(rows_ready, 1)
            cmp_rows = a["cache_kv_cmp"].rearrange("n (c s) k g d -> (n c) (s k g d)", s=8)
            slc_rows = a["cache_kv_slc"].rearrange("n t k g d -> (n t k) (g d)")
            for n, (kind, arg, _, count) in enumerate(PLAN):
                if count == 0:
                    continue
                pool.wait_ge(slab_used, n - NS + 1)
                if kind == "cmp":
                    b, half = arg
                    pool.indirect_dma_start(slab(n), None, cmp_rows, bass.IndirectOffsetOnAxis(
                        ap=row_cmp[:, half, b:b + 1], axis=0)).then_inc(rows_in[n % NS], 16)
                    continue
                kv = int(kind == "vpage")
                dst = slab(n).rearrange("p (x c) -> p x c", x=16)
                for x in range(1, 16, 2):
                    at = slab_page(kind, arg, x)
                    pool.indirect_dma_start(dst[:, x, :], None, slc_rows, bass.IndirectOffsetOnAxis(
                        ap=row_kv[:, kv, at:at + 1], axis=0)).then_inc(rows_in[n % NS], 16)
            pool.wait_ge(od_full, 1)
            pool.dma_start(a["kv_win_sample"][:, 0:WIN - 1].rearrange("b t k g d -> b (t k g d)"),
                           a["state_kv_win"][:, 1:WIN].rearrange("b t k g d -> b (t k g d)")).then_inc(copies, 16)
            nc.gpsimd.memset(KZ[64:128, 0, :, :], 0.0)
            nc.gpsimd.memset(KZ[0:64, 1, :, :], 0.0).then_inc(kz_ready, 1)
            for n in range(NTK):
                pool.wait_ge(as_rec, n + 1)
                for i, x, r, bank, c0 in softmaxes(n):
                    if r == 0:
                        ins = scale_probs(nc.gpsimd, n, i, x, r, bank, c0)
                ins.then_inc(as_p, 1)
            pool.wait_ge(copies, 16)

        @block.scalar
        def _(act):
            n_ch = [0]

            def link(ins):
                n_ch[0] += 1
                ins.then_inc(act_ch, 1)
                act.wait_ge(act_ch, n_ch[0])

            def root(c0, c1, rows):
                return nc.scalar.activation(ssq[0:rows, c0:c1], ssq[0:rows, c0:c1], ACT.Sqrt, scale=1.0 / D,
                                            bias=epsb[0:rows, :])

            def rms(src, junk_, ready):
                for t, r in enumerate(ROWS):
                    ready(t)
                    link(nc.scalar.activation(junk_[0:r, :], src[0:r, t, :], ACT.Square,
                                              accum_out=ssq[0:r, t:t + 1]))
                    root(t, t + 1, r).then_inc(root_ready, 1)

            act.wait_ge(masks_ready, 1)
            rms(xtm, junk, lambda t: act.wait_ge(x_in[t], 16))

            act.wait_ge(par_in, 16 * N_PAR)
            nc.scalar.activation(dt, ldt, ACT.Exp).then_inc(ldt_ready, 1)
            act.wait_ge(ang_ready, 1)
            nc.scalar.activation(mag, mag, ACT.Exp)
            nc.scalar.activation(sn, ang2, ACT.Sin)
            nc.scalar.activation(sh, ang2, ACT.Sin, scale=0.5).then_inc(trig_ready, 1)
            act.wait_ge(zero_ready, 2)
            for r, name in enumerate(("s5_c_re", "s5_c_im")):
                for ii in range(4):
                    for g in range(2):
                        row = 32 * ii + 16 * g
                        act.dma_start(CCP[row:row + C5, r, ii:NST:4, 64 * g:64 * g + 64],
                                      a[name].rearrange("(q i g) c n -> i g c q n", q=4, g=2)[ii, g]
                                      ).then_inc(c_in, 16)

            nkv = 0
            for u, unit in enumerate(HEAD_UNITS + REST_UNITS):
                act.wait_ge(pair_full, u + 1)
                kind = unit[0]
                pr = pair(u)
                if kind == "gemm" and unit[4][0] != "gn":
                    to = unit[4]
                    scale = 1.0
                    if to[0] == "u":
                        dst = uT[:, to[1], :]
                    elif to[0] == "q":
                        dst = qT[:, to[1], :]
                        scale = DH ** -0.5
                        if to[1] == 4:
                            for s_ in kv_store:
                                act.wait_ge(s_, 16 * len(KV_TILES) // 4)
                    elif to[1] > 0 and to[2] < 2:
                        dst = kT[:, 2 * (to[1] - 1) + to[2], :]
                    else:
                        dst = zst[:, to[2] % 2, :]
                    ins = nc.scalar.activation(halves(dst), pr[:, :, 0:HALF], ACT.Copy, scale=scale)
                elif kind == "gemm":
                    nc.scalar.activation(gsT[:, 0:HALF], pr[0:3 * NH, 0, 0:HALF], ACT.Sigmoid)
                    nc.scalar.activation(gsT[:, HALF:T], pr[0:3 * NH, 1, 0:T - HALF], ACT.Sigmoid)
                    ins = nc.scalar.activation(gsTs[0:3 * NH, :], pr[0:3 * NH, 1, T - HALF:HALF], ACT.Sigmoid)
                elif kind == "tr":
                    c, m = unit[1:]
                    if nkv >= 4:
                        act.wait_ge(kv_store[nkv % 4], 16 * (nkv // 4))
                    if c > 0 and m >= 2:
                        dst = vtm[:, :, 256 * (c - 1) + P * (m - 2):256 * (c - 1) + P * (m - 1)]
                    else:
                        dst = kst[:, nkv % 4]
                    nc.scalar.activation(kvs[:, KVW * c + P * m:KVW * c + P * m + P], pr[0:NB, 1, 0:P], ACT.Copy)
                    nc.scalar.activation(dst, pr[:, 0, :].rearrange("p (t c) -> p t c", t=TT),
                                         ACT.Copy).then_inc(pair_free, 1)
                    act.wait_ge(pair_free, u + 1)
                    name = ("kv_cmp_prompt", "kv_slc_prompt", "kv_win_prompt")[c]
                    out = a[name].rearrange("o (t p) k g d -> p (o t) (k g d)", p=P)[:, :, P * m:P * m + P]
                    act.dma_start(out, dst).then_inc(kv_store[nkv % 4], 16)
                    nkv += 1
                    continue
                elif kind == "trg":
                    nc.scalar.activation(gs8[0:NB, :], pr[0:NB, 1, 0:3 * NH], ACT.Copy)
                    ins = nc.scalar.activation(gtm[:, :, :],
                                               pr[:, 0, 0:TT * 3 * NH].rearrange("p (t c) -> p t c", t=TT), ACT.Copy)
                elif kind in ("bb", "cc"):
                    _, ri, q = unit
                    ins = nc.scalar.activation((BBT if kind == "bb" else CCT)[:, ri, 4 * q:4 * q + 4, :],
                                               pr[:, 0, :].rearrange("p (i c) -> p i c", i=4), ACT.Copy,
                                               scale=-1.0 if kind == "cc" and ri else 1.0)
                else:
                    ins = nc.scalar.activation(h0T if kind == "h0" else buS,
                                               pr[:, 0, 0:256].rearrange("p (i r b) -> p i r b", i=NST, r=2), ACT.Copy)
                ins.then_inc(pair_free, 1)

            for v in range(8):
                act.wait_ge(st_full, v + 1)
                src = PS[0:9, v % 2, :].rearrange("p (i r c) -> p i r c", i=2, r=2)
                for r in range(2):
                    ins = nc.scalar.activation(STO[:, 2 * v:2 * v + 2, :, r], src[:, :, r, :], ACT.Copy)
                ins.then_inc(st_ready, 1)
            act.wait_ge(st_ready, 8)
            flat = QO[0:9, KD * NT:KD * NT + 4096]
            act.dma_start(a["s5_prompt"].rearrange("b g n r -> b (g n r)"), flat[0:1]).then_inc(s5_store, 16)
            act.dma_start(a["s5_sample"].rearrange("b g n r -> b (g n r)"), flat[1:9]).then_inc(s5_store, 16)
            for c, name in enumerate(("kv_cmp_sample", "kv_slc_sample")):
                act.dma_start(a[name].rearrange("b o k g d -> (b o) (k g d)"),
                              kvs[:, KVW * c:KVW * c + KVW]).then_inc(stores, 16)
            act.dma_start(a["kv_win_sample"].rearrange("b t k g d -> b t (k g d)")[:, WIN - 1, :],
                          kvs[:, 2 * KVW:3 * KVW]).then_inc(stores, 16)
            def xt_evac(r, w):
                act.wait_ge(xt_full, r + 1)
                if r >= 3:
                    act.wait_ge(xt_used, r - 2)
                bank = 4 + r % 3 if r < N_RS else 6 + (r - N_RS) % 2
                nc.scalar.activation(XT[:, r % 3, 0:w], PS[:, bank, 0:w], ACT.Copy).then_inc(xt_ready, 1)

            def gelu(b):
                w = 4 * (NC if b < NB else NCP)
                act.wait_ge(pre_ready, b + 1)
                if b:
                    act.wait_ge(l2_full, b)
                nc.scalar.activation(GEL[:, 0:w], PRE[:, 0:w], ACT.Gelu_apprx_tanh).then_inc(gelu_ready, 1)

            for r, (b, half, kind, s4) in enumerate(RS):
                xt_evac(r, 4 * (NCH if b < NB else NCP + 1))
                if b and r % 16 == 3:
                    gelu(b - 1)
            gelu(NB)
            act.wait_ge(l2_full, NB + 1)
            act.dma_start(R[0:32, 2625:3714], a["tie"].rearrange("p j i -> p (j i)")).then_inc(tie_in, 16)

            for r in range(len(KR)):
                xt_evac(N_RS + r, 512)
                if r == 15:
                    act.wait_ge(sc_max, 1)
                    nc.scalar.activation(SC[:, 0:NC], SC[:, 0:NC], ACT.Exp, bias=dmx[:, 0:1],
                                         accum_out=dsm[:, 0:1]).then_inc(sc_exp, 1)
                if r in R_CE:
                    t = R_CE.index(r)
                    act.wait_ge(cs_max, t + 1)
                    nc.scalar.activation(PCP[:, t], PCP[:, t], ACT.Exp).then_inc(cs_exp, 1)
                if r == R_SA:
                    act.wait_ge(samax, 1)
                    nc.scalar.activation(SA, SA, ACT.Exp, bias=dmx[:, 1:2], accum_out=dsm[:, 1:2]
                                         ).then_inc(saexp, 1)
            act.wait_ge(smax, 1)
            nc.scalar.activation(SW[:, 1:513], SW[:, 1:513], ACT.Exp, bias=dmx[:, 2:3],
                                 accum_out=dsm[:, 2:3]).then_inc(sexp, 1)
            for v in range(6):
                act.wait_ge(pt_full, v + 1)
                bank = PT_BANK[v]
                if v < 5:
                    ins = nc.scalar.activation(PTA[:, 4 * v:4 * v + 4, :],
                                               PS[:, bank, :].rearrange("p (g c) -> p g c", g=4), ACT.Copy)
                else:
                    nc.scalar.activation(PTC[0:NC, :], PS[0:NC, bank, 0:P], ACT.Copy)
                    ins = nc.scalar.activation(PTN, PS[0:NB, bank, P:3 * P].rearrange("p (r c) -> p r c", r=2),
                                               ACT.Copy)
                ins.then_inc(pt_ready, 1)

            act.wait_ge(od_full, 1)
            for j in range(2):
                ins = nc.scalar.activation(KZ[64 * j:64 * j + 64, j], kT[64 * j:64 * j + 64, :, 0:T], ACT.Copy)
            ins.then_inc(kz_ready, 1)
            for n in range(NTK + 1):
                if n < NTK:
                    t = TASKS[n][0]
                    act.wait_ge(as_max, n + 1)
                    if n >= 2:
                        act.wait_ge(at_full, n - 1)
                    for i, x, r, bank, c0 in softmaxes(n):
                        k = 4 * (n % 2) + i
                        ins = nc.scalar.activation(PP[:, n % 2, bank, c0:c0 + P * (t + 1)],
                                                   PS[:, 1 + 2 * (n % 2) + bank, c0:c0 + P * (t + 1)], ACT.Exp,
                                                   bias=amx[:, k:k + 1], accum_out=asm[:, k:k + 1])
                    ins.then_inc(as_exp, 1)
                if n >= 1:
                    m = n - 1
                    t = TASKS[m][0]
                    act.wait_ge(at_full, m + 1)
                    if m >= 2:
                        act.wait_ge(ao_full, m - 1)
                    nc.scalar.activation(blocks(m, PTP[:, m % 2, 0, :], P * (t + 1)),
                                         blocks(m, PS[:, 5, :], P * (t + 1)), ACT.Copy).then_inc(at_a, 1)

            act.wait_ge(ao_free, NTK)
            for q in range(4):
                ins = nc.scalar.activation(zT[:, q, :], uT[:, q, :], ACT.Gelu_apprx_tanh)
            ins.then_inc(z_ready, 1)
            for m in range(4):
                u = U_GLU + m
                act.wait_ge(pair_full, u + 1)
                if m >= 2:
                    act.wait_ge(os5_ready, m - 1)
                nc.scalar.activation(halves(sgl[:, m % 2, :]), pair(u)[:, :, 0:HALF], ACT.Sigmoid,
                                     bias=bglu[:, m:m + 1]).then_inc(pair_free, 1)
            for m in range(KD):
                for w in range(4):
                    u = U_MIX + 4 * m + w
                    act.wait_ge(pair_full, u + 1)
                    if m >= 2 and w == 0:
                        act.wait_ge(mix_ready, m - 1)
                    nc.scalar.activation(halves(mxb[:, m % 2, w, :]), pair(u)[:, :, 0:HALF],
                                         ACT.Sigmoid if w < 2 else ACT.Copy).then_inc(pair_free, 1)

            act.dma_start(x1[:, 0:TT, :], a["x_prompt"].rearrange("o (t p) d -> p (o t) d", p=P)).then_inc(x2_in, 16)
            act.dma_start(x1[0:NB, TT, :], a["x_sample"].rearrange("b o d -> (b o) d")).then_inc(x2_in, 16)
            act.dma_start(gain, a["norm_mix_post"].rearrange("(o d) -> o d", o=1).to_broadcast([P, D])
                          ).then_inc(gain_in, 16)

            def out_units(base, stage, which):
                for i, (kind, m) in enumerate(OUT_ORDER):
                    u = base + i
                    if kind == "g":
                        act.wait_ge(pair_full, u + 1)
                    pr = pair(u)
                    if kind == "g":
                        ins = nc.scalar.activation(halves(stage[:, m % 2, :]), pr[:, :, 0:HALF], ACT.Copy)
                    else:
                        act.wait_ge(yg_ready, KD * which + m + 1)
                        act.wait_ge(pair_free, u)
                        for t in range(TT):
                            nc.scalar.activation(sqj[:, t, :], pr[:, 0, P * t:P * t + P], ACT.Square,
                                                 accum_out=sqm[:, t, m:m + 1])
                        ins = nc.scalar.activation(sqj[0:NB, TT, :], pr[0:NB, 1, 0:P], ACT.Square,
                                                   accum_out=sqm[0:NB, TT, m:m + 1])
                    ins.then_inc(pair_free, 1)
                act.wait_ge(ssq_ready, which + 1)
                root(0, TT, P)
                root(TT, TT + 1, NB).then_inc(root_ready, 1)

            out_units(U_OUT, zo, 0)
            rms(x1, R[:, 0:D], lambda t: act.wait_ge(x1_ready, t + 1))
            act.dma_start(gain, a["norm_mlp_post"].rearrange("(o d) -> o d", o=1).to_broadcast([P, D])
                          ).then_inc(gain_in, 16)
            for m in range(KF):
                u = U_UP + m
                act.wait_ge(pair_full, u + 1)
                nc.scalar.activation(halves(fT[:, m, :]), pair(u)[:, :, 0:HALF], ACT.Relu).then_inc(pair_free, 1)
            out_units(U_DOWN, hT, 1)
            for t in range(5):
                act.wait_ge(x1_ready, 6 + t)
                if t < TT:
                    act.dma_start(a["y_prompt"][0, P * t:P * t + P, :], x1[:, t, :]).then_inc(stores, 16)
                else:
                    act.dma_start(a["y_sample"].rearrange("b o d -> (b o) d"), x1[0:NB, TT, :]).then_inc(stores, 16)
            act.wait_ge(stores, 16 * 8)

        @block.vector
        def _(dve):
            n_ch = [0]

            def link(ins):
                n_ch[0] += 1
                ins.then_inc(dve_ch, 1)
                dve.wait_ge(dve_ch, n_ch[0])

            V = nc.vector
            V.memset(epsb, EPS)
            dve.wait_ge(consts_in, 16)
            V.tensor_copy(idb[:, :], ident)
            V.tensor_copy(maskb[:, :], consts[:, CO_MASK:CO_MASK + P]).then_inc(masks_ready, 1)

            def pre_norm(first, src, dst, gains, roots, make=None):
                def evac(t):
                    for half in range(2):
                        v = first + 2 * t + half
                        w = ROWS[t]
                        dve.wait_ge(xnt_full, v + 1)
                        V.tensor_tensor(hT[:, 4 * half:4 * half + 4, P * t:P * t + w],
                                        PS[:, 4 + v % 4, 0:4 * w].rearrange("p (k c) -> p k c", k=4),
                                        gains[:, 4 * half:4 * half + 4].unsqueeze(2).to_broadcast([P, 4, w]),
                                        ALU.mult).then_inc(xnt_free, 1)

                if make:
                    make(0)
                for t, r in enumerate(ROWS):
                    if make and t + 1 < len(ROWS):
                        make(t + 1)
                    dve.wait_ge(root_ready, roots + t + 1)
                    link(V.reciprocal(rstd[0:r, t:t + 1], ssq[0:r, t:t + 1]))
                    if t >= 2:
                        dve.wait_ge(xnt_full, first + 2 * (t - 1))
                    V.tensor_scalar(dst[0:r, t % 2, :], src[0:r, t, :], rstd[0:r, t:t + 1], None,
                                    ALU.mult).then_inc(xn_ready, 1)
                    if t:
                        evac(t - 1)
                evac(4)

            dve.wait_ge(g_in, 32)
            pre_norm(0, xtm, xn, gT[:, 0, :], 0)
            dve.wait_ge(par_in, 16 * N_PAR)

            dve.wait_ge(pages_in, 16 * (1 + N_PAGES))
            link(V.tensor_scalar(row_kv[:, 0], pages[:, :], 2.0 * PAGE, consts[:, CO_ROW:CO_ROW + 1], ALU.mult, ALU.add))
            V.tensor_scalar(row_kv[:, 1], row_kv[:, 0], 1.0, None, ALU.add)
            link(V.tensor_scalar(row_cmp[:, 0], pages8[:, :], 16.0, consts[:, CO_ROW + 1:CO_ROW + 2],
                                 ALU.mult, ALU.add))
            V.tensor_scalar(row_cmp[:, 1], row_cmp[:, 0], 1.0, None, ALU.add).then_inc(rows_ready, 1)

            dve.wait_ge(ldt_ready, 1)
            V.tensor_tensor(mag, are, dt, ALU.mult)
            link(V.tensor_tensor(ang, aim, dt, ALU.mult))
            link(V.tensor_scalar(s5t, ang, 1.0 / TWO_PI, None, ALU.mult))
            link(V.tensor_scalar(s5t, s5t, RND, RND, ALU.add, ALU.subtract))
            link(V.scalar_tensor_tensor(ang2, s5t, -6.28125, ang, ALU.mult, ALU.add))
            link(V.scalar_tensor_tensor(ang2, s5t, -(TWO_PI - 6.28125), ang2, ALU.mult, ALU.add))
            V.tensor_scalar(ang2, ang2, 3.1415925, -3.1415925, ALU.min, ALU.max).then_inc(ang_ready, 1)
            dve.wait_ge(trig_ready, 1)
            link(V.tensor_tensor(s5t, sh, sh, ALU.mult))
            link(V.tensor_scalar(cs, s5t, -2.0, 1.0, ALU.mult, ALU.add))
            link(V.tensor_tensor(abr, mag, cs, ALU.mult))
            link(V.tensor_tensor(abi, mag, sn, ALU.mult))
            V.tensor_scalar(nabi, abi, -1.0, None, ALU.mult).then_inc(unit_ready, 1)
            link(V.tensor_tensor(den, are, are, ALU.mult))
            link(V.tensor_tensor(s5t, aim, aim, ALU.mult))
            link(V.tensor_tensor(den, den, s5t, ALU.add))
            link(V.reciprocal(den, den))
            link(V.tensor_scalar(s5u, abr, -1.0, None, ALU.add))
            link(V.tensor_tensor(cor, s5u, are, ALU.mult))
            link(V.tensor_tensor(s5t, abi, aim, ALU.mult))
            link(V.tensor_tensor(cor, cor, s5t, ALU.add))
            link(V.tensor_tensor(cor, cor, den, ALU.mult))
            link(V.tensor_tensor(coi, abi, are, ALU.mult))
            link(V.tensor_tensor(s5t, s5u, aim, ALU.mult))
            link(V.tensor_tensor(coi, coi, s5t, ALU.subtract))
            link(V.tensor_tensor(coi, coi, den, ALU.mult))
            CR, CI = (x.unsqueeze(2).to_broadcast([P, NST, C5]) for x in (cor, coi))
            V.tensor_tensor(bwk[:, 0], bld[:, 0], CR, ALU.mult)
            V.tensor_tensor(bwk[:, 1], bld[:, 1], CI, ALU.mult)
            V.tensor_tensor(bwk[:, 2], bld[:, 0], CI, ALU.mult)
            link(V.tensor_tensor(bwk[:, 3], bld[:, 1], CR, ALU.mult))
            dve.wait_ge(zero_ready, 1)
            for r, op in ((0, ALU.subtract), (1, ALU.add)):
                for ii in range(4):
                    for g in range(2):
                        rows, col = slice(64 * g, 64 * g + 64), 32 * ii + 16 * g
                        ins = V.tensor_tensor(BBP[rows, r, ii:NST:4, col:col + C5], bwk[rows, 2 * r, ii:NST:4, :],
                                              bwk[rows, 2 * r + 1, ii:NST:4, :], op)
            ins.then_inc(bb_ready, 1)

            def y_evac(q):
                dve.wait_ge(y_full, q + 1)
                V.scalar_tensor_tensor(uT[:, q, 0:T], uT[:, q, 0:T], s5d[:, q:q + 1], PS[:, 6, 0:T],
                                       ALU.mult, ALU.add)
                V.scalar_tensor_tensor(uT[:, q, T:NT], uT[:, q, T:NT], s5d[:, q:q + 1], PS[:, 7, 0:NB],
                                       ALU.mult, ALU.add).then_inc(y_free, 1)

            t1, t2, xr, xi = (w[:, 0:T] for w in W5[0:4])
            for i in range(NST):
                if i % 4 == 0:
                    dve.wait_ge(table_ready, i // 4 + 1)
                if i == 0:
                    dve.wait_ge(pair_free, 22)
                ct, st = TAB[:, (i // 4) % 2, 0, i % 4, :], TAB[:, (i // 4) % 2, 1, i % 4, :]
                hr, hi = W5[4 + 2 * (i % 2)], W5[5 + 2 * (i % 2)]
                dve.wait_ge(bu_full, i + 1)
                br, bi = PS[:, 4, :], PS[:, 5, :]
                V.tensor_tensor(t1, br, ct, ALU.mult)
                link(V.tensor_tensor(t2, bi, st, ALU.mult))
                V.tensor_tensor(xr, t1, t2, ALU.add)
                link(V.tensor_tensor(xi, bi, ct, ALU.mult))
                V.tensor_tensor(t2, br, st, ALU.mult).then_inc(bu_free, 1)
                dve.wait_ge(bu_free, i + 1)
                r = mag[:, i:i + 1].to_broadcast([P, T])
                link(V.tensor_tensor(xi, xi, t2, ALU.subtract))
                V.tensor_tensor_scan(xr, r, xr, 0.0, ALU.mult, ALU.add)
                link(V.tensor_tensor_scan(xi, r, xi, 0.0, ALU.mult, ALU.add))
                if i >= 2:
                    dve.wait_ge(h_used, i - 1)
                V.tensor_tensor(hr[:, 0:T], ct, xr, ALU.mult)
                link(V.tensor_tensor(t2, st, xi, ALU.mult))
                V.tensor_tensor(hr[:, 0:T], hr[:, 0:T], t2, ALU.subtract)
                V.tensor_tensor(hi[:, 0:T], st, xr, ALU.mult)
                link(V.tensor_tensor(t1, ct, xi, ALU.mult))
                V.tensor_tensor(hi[:, 0:T], hi[:, 0:T], t1, ALU.add)
                V.scalar_tensor_tensor(sst[:, 0], h0T[:, i, 0], abr[:, i:i + 1], buS[:, i, 0], ALU.mult, ALU.add)
                link(V.scalar_tensor_tensor(sst[:, 1], h0T[:, i, 1], abr[:, i:i + 1], buS[:, i, 1],
                                            ALU.mult, ALU.add))
                V.scalar_tensor_tensor(hr[:, T:NT], h0T[:, i, 1], nabi[:, i:i + 1], sst[:, 0], ALU.mult, ALU.add)
                link(V.scalar_tensor_tensor(hi[:, T:NT], h0T[:, i, 0], abi[:, i:i + 1], sst[:, 1],
                                            ALU.mult, ALU.add))
                V.tensor_copy(hS[:, i, 0], hr[:, T - 1:NT])
                V.tensor_copy(hS[:, i, 1], hi[:, T - 1:NT]).then_inc(h_ready, 1)
                if i % 4 == 0 and i:
                    y_evac(i // 4 - 1)
            y_evac(3)

            def permute(w):
                b, half, kind = w // 4, w // 2 % 2, w % 2
                n = NCH if b < NB else NCP + 1
                s = SLAB[("cmp", (b, half))]
                if kind == 0:
                    wait_slab(dve, s)
                if w >= 3:
                    dve.wait_ge(xt_full, 4 * (w - 2))
                V.tensor_copy(ROWSP[0:n, w % 3], slab(s)[0:n].rearrange("p (s k g d) -> p k g s d", s=8, k=2, g=4)
                              [:, kind]).then_inc(perm_ready, 1)

            permute(0)
            permute(1)
            dve.wait_ge(pos_full, 1)
            V.tensor_copy(pos[0:64], PS[0:64, 7, 0:1])
            link(V.tensor_copy(pos[64:128], PS[0:64, 7, 1:2]))
            permute(2)
            permute(3)
            for b in range(NB + 1):
                if b < NB:
                    permute(4 * b + 4)
                    permute(4 * b + 5)
                n = NCH if b < NB else NCP + 1
                k4 = PS[:, 2 * (b % 2), 0:4 * n].rearrange("p (g n) -> p g n", g=4)
                v4 = PS[:, 2 * (b % 2) + 1, 0:4 * n].rearrange("p (g n) -> p g n", g=4)
                sh4 = SH[:, 0:4 * n].rearrange("p (g n) -> p g n", g=4)
                pr4 = PRE[:, 0:4 * (n - 1)].rearrange("p (g n) -> p g n", g=4)
                dve.wait_ge(acc_full, b + 1)
                V.tensor_copy(SH[0:64, 0:4 * n], PS[64:128, 2 * (b % 2), 0:4 * n])
                link(V.tensor_copy(SH[64:128, 0:4 * n], PS[0:64, 2 * (b % 2) + 1, 0:4 * n]))
                if b:
                    dve.wait_ge(gelu_ready, b)
                for rows, acc in ((slice(0, 64), k4), (slice(64, 128), v4)):
                    ins = V.scalar_tensor_tensor(pr4[rows], acc[rows][:, :, 0:n - 1], pos[rows, 0:1],
                                                 sh4[rows][:, :, 1:n], ALU.add, ALU.add)
                ins.then_inc(pre_ready, 1)
                if b < NB:
                    permute(4 * b + 6)
                dve.wait_ge(l2_full, b + 1)
                if b < NB:
                    for j in range(2):
                        V.tensor_copy(kcT[64 * j:64 * j + 64, b, :, 0:NC],
                                      PS[0:64, 2 * (b % 2), 0:4 * NC].rearrange("p (q j n) -> p q j n", q=2, j=2)
                                      [:, :, j, :])
                else:
                    link(V.memset(KCZ, 0.0))
                    for j in range(2):
                        V.tensor_copy(KCZ[64 * j:64 * j + 64, :, j, :],
                                      PS[0:64, 2 * (b % 2), 0:4 * NCP].rearrange("p (q j n) -> p q j n", q=2, j=2)
                                      [:, :, j, :])
                V.tensor_copy(vc[0:n - 1, b, :], PS[0:n - 1, 2 * (b % 2) + 1, 0:256]).then_inc(l2_ready, 1)
                if b < NB:
                    permute(4 * b + 7)
                else:
                    link(V.memset(QP[:, :, :, :], 0.0))
                    for p in range(2):
                        flat = QP[:, p].rearrange("p b c -> p (b c)")
                        for j in range(2):
                            for h in range(HPG):
                                c0 = 8 * p + 4 * j + h
                                ins = V.tensor_copy(flat[64 * j:64 * j + 64, c0:c0 + 144 * 7 + 1:144],
                                                    qT[64 * j:64 * j + 64, 4 * p + h, T:NT])
                    for r in range(2):
                        ins = V.tensor_copy(kcT[:, :, :, NC + r], kT[:, 2 * r:2 * r + 2, T:NT].rearrange("p q b -> p b q"))
                    ins.then_inc(qpad_ready, 1)

            def compressed(t):
                dve.wait_ge(cs_full, t + 1)
                for j in range(2):
                    ins = V.tensor_tensor(PCP[:, t].rearrange("p (q j h) n -> p j q h n", q=2, j=2)[:, j],
                                          PS[:, 5, 0:NH * NCP].rearrange("p (q h j n) -> p j q h n", q=2, h=HPG, j=2)
                                          [:, j],
                                          consts[:, CO_CMASK + NCP * t:CO_CMASK + NCP * (t + 1)].unsqueeze(1)
                                          .unsqueeze(1).to_broadcast([P, 2, HPG, NCP]), ALU.add)
                link(ins)
                link(V.reduce_max(cmx, PCP[:, t], AX))
                V.tensor_tensor(PCP[:, t], PCP[:, t], cmx.unsqueeze(2).to_broadcast([P, NH, NCP]),
                                ALU.subtract).then_inc(cs_max, 1)
                dve.wait_ge(cs_exp, t + 1)
                link(V.reduce_sum(csm, PCP[:, t], AX))
                link(V.reciprocal(csm, csm))
                link(V.scalar_tensor_tensor(csm, csm, consts[:, CO_ROWV + t:CO_ROWV + t + 1],
                                            gtm[:, t, 0:3 * NH:3], ALU.mult, ALU.mult))
                link(V.tensor_tensor(PCP[:, t], PCP[:, t], csm.unsqueeze(2).to_broadcast([P, NH, NCP]), ALU.mult))

            def selected(q):
                dve.wait_ge(s_full, q + 1)
                link(V.tensor_tensor(SA[:, 512 * q:512 * q + 512].rearrange("p (j t) -> p j t", t=SELB),
                                     PS[:, q, :].rearrange("p (j t) -> p j t", t=SELB),
                                     SELX[:, 8 * q:8 * q + 8].unsqueeze(2).to_broadcast([P, 8, SELB]), ALU.add))
                link(V.reduce_max(pmx[:, q:q + 1], SA[:, 512 * q:512 * q + 512 + (q == 3)], AX))

            dve.wait_ge(sc_full, 1)
            V.tensor_tensor(GH.rearrange("p (h r) -> p h r", r=3),
                            PS[:, 4, 0:48].rearrange("p (h r) -> p h r", r=3),
                            consts[:, CO_HM:CO_HM + NH].unsqueeze(2).to_broadcast([P, NH, 3]), ALU.mult)
            link(V.tensor_copy(SC, PS[:, 5, 0:129]))
            V.tensor_reduce(gd, GH.rearrange("p (h r) -> p r h", r=3), AX, ALU.add)
            V.reduce_max(dmx[:, 0:1], SC[:, 0:NC], AX, negate=True).then_inc(sc_max, 1)
            dve.wait_ge(sc_exp, 1)
            link(V.reciprocal(dinv[:, 0:1], dsm[:, 0:1]))
            V.tensor_scalar(SC[:, 0:NC], SC[:, 0:NC], dinv[:, 0:1], None, ALU.mult).then_inc(pc_ready, 1)
            link(V.memset(IMP, 0.0))
            dve.wait_ge(imp_full, 1)
            link(V.tensor_copy(IMP[:, 1:NC + 1], PS[0:32, 5, 0:NC]))
            link(V.tensor_reduce(SSEL, IMP[:, 0:132].rearrange("p (j k) -> p j k", k=4), AX, ALU.add))
            link(V.tensor_tensor(SSEL, SSEL, IMP[:, 4:133:4], ALU.add))
            V.memset(SSEL[:, 0:1], FORCE)
            link(V.memset(SSEL[:, NSEL - 2:NSEL], FORCE))
            Si = SSEL.unsqueeze(1).to_broadcast([32, NSEL, NSEL])
            Sj = SSEL.unsqueeze(2).to_broadcast([32, NSEL, NSEL])
            dve.wait_ge(tie_in, 16)
            V.tensor_tensor(CMPA, Si, Sj, ALU.is_gt)
            link(V.tensor_tensor(CMPB, Si, Sj, ALU.is_equal))
            link(V.tensor_tensor(CMPB, CMPB, TIE, ALU.mult))
            link(V.tensor_tensor(CMPA, CMPA, CMPB, ALU.add))
            link(V.tensor_reduce(SSEL, CMPA, AX, ALU.add))
            V.tensor_scalar(SSEL, SSEL, float(TOPK), None, ALU.is_lt).then_inc(sel_ready, 1)
            dve.wait_ge(selx_full, 1)
            V.tensor_scalar(SELX, PS[:, 5, 0:NSEL], 1.0, -NEG, ALU.subtract, ALU.mult).then_inc(selx_read, 1)
            dve.wait_ge(selx_read, 1)
            link(V.tensor_tensor(SA[:, 2048:2049], SC[:, NC:NC + 1], SELX[:, NSEL - 1:NSEL], ALU.add))
            compressed(0)
            selected(0)
            selected(1)
            compressed(1)
            selected(2)
            compressed(2)
            selected(3)
            V.reduce_max(dmx[:, 1:2], pmx, AX, negate=True).then_inc(samax, 1)
            compressed(3)
            dve.wait_ge(saexp, 1)
            link(V.reciprocal(dinv[:, 1:2], dsm[:, 1:2]))
            link(V.tensor_tensor(dinv[:, 1:2], dinv[:, 1:2], gd[:, 1:2], ALU.mult))
            link(V.tensor_scalar(SA, SA, dinv[:, 1:2], None, ALU.mult))
            V.tensor_scalar(SC[:, 0:NC], SC[:, 0:NC], gd[:, 0:1], None, ALU.mult)
            V.tensor_scalar(PNB[:, 0], consts[:, CO_BM:CO_BM + NB], SA[:, 2048:2049], None,
                            ALU.mult).then_inc(pa_ready, 1)
            dve.wait_ge(s_full, 5)
            V.tensor_copy(SW[:, 512:513], SC[:, NC + 1:NC + 2])
            link(V.tensor_copy(SW[:, 0:512], PS[:, 4, :]))
            V.reduce_max(dmx[:, 2:3], SW[:, 1:513], AX, negate=True).then_inc(smax, 1)
            dve.wait_ge(sexp, 1)
            link(V.reciprocal(dinv[:, 2:3], dsm[:, 2:3]))
            link(V.tensor_tensor(dinv[:, 2:3], dinv[:, 2:3], gd[:, 2:3], ALU.mult))
            V.memset(SW[:, 0:1], 0.0)
            link(V.tensor_scalar(SW[:, 1:513], SW[:, 1:513], dinv[:, 2:3], None, ALU.mult))
            V.tensor_scalar(PNB[:, 1], consts[:, CO_BM:CO_BM + NB], SW[:, 512:513], None,
                            ALU.mult).then_inc(p_ready, 1)
            own = consts[0:NH, CO_GM16:CO_GM16 + 4 * NB].unsqueeze(2).to_broadcast([NH, 4 * NB, DH])
            dve.wait_ge(oe_full, 1)
            V.tensor_tensor(OE, PS[0:NH, 4:8, :].rearrange("p b (x d) -> p (b x) d", d=DH), own, ALU.mult)
            dve.wait_ge(od_full, 1)
            V.tensor_tensor(OD, PS[0:NH, 0:4, :].rearrange("p b (x d) -> p (b x) d", d=DH), own,
                            ALU.mult).then_inc(od_ready, 1)
            dve.wait_ge(od_ready, 1)
            link(V.tensor_tensor(OD, OD, OE, ALU.add))
            V.tensor_reduce(OS, OD.rearrange("p (b g) d -> p b d g", g=NG), AX, ALU.add).then_inc(ot_ready, 1)

            dve.wait_ge(ot_full, 1)
            dve.wait_ge(s5_store, 32)
            for p in range(2):
                for j in range(2):
                    ins = V.tensor_copy(oT[64 * j:64 * j + 64, 4 * p:4 * p + 4, T:NT],
                                        PS[0:DH, 7, 0:P].rearrange("p (b x) -> p x b", x=NH)
                                        [:, 8 * p + 4 * j:8 * p + 4 * j + 4, :])
            ins.then_inc(ot_done, 1)
            for n in range(NTK + 2):
                if n < NTK:
                    t = TASKS[n][0]
                    dve.wait_ge(as_full, n + 1)
                    k, bank, nx = 4 * (n % 2), 1 + 2 * (n % 2), TASKS[n][4]
                    S = PS[:, bank:bank + 2, :]
                    if nx == 2:
                        S = S.rearrange("p x (r c) -> p (x r) c", r=2)
                    V.reduce_max(amx[:, k:k + 2 * nx], S[:, :, 0:P * (t + 1)], AX, negate=True).then_inc(as_max, 1)
                if 1 <= n <= NTK:
                    m = n - 1
                    t = TASKS[m][0]
                    dve.wait_ge(at_full, m + 1)
                    if m >= 2:
                        dve.wait_ge(ao_full, m - 1)
                    w = P * TASKS[m][4]
                    V.tensor_copy(PTPC[0:NCP, m % 2, 0:w], PS[0:NCP, 0, 0:w])
                    V.tensor_copy(blocks(m, PTP[:, m % 2, 1, :], P * (t + 1)),
                                  blocks(m, PS[:, 6, :], P * (t + 1))).then_inc(at_d, 1)
                if n >= 2:
                    t, p, h, j, nx = TASKS[n - 2]
                    dve.wait_ge(ao_full, n - 1)
                    V.tensor_copy(oT[64 * j:64 * j + 64, 4 * p + h:4 * p + h + nx, P * t:P * t + P],
                                  PS[0:64, 7, 0:P * nx].rearrange("p (x c) -> p x c", x=nx)).then_inc(ao_free, 1)
                if n < NTK:
                    dve.wait_ge(as_exp, n + 1)
                    k, nx = 4 * (n % 2), TASKS[n][4]
                    V.reciprocal(ainv[:, k:k + 2 * nx], asm[:, k:k + 2 * nx]).then_inc(as_rec, 1)
                    dve.wait_ge(as_rec, n + 1)
                    for i, x, r, bank, c0 in softmaxes(n):
                        if r == 1:
                            ins = scale_probs(V, n, i, x, r, bank, c0)
                    ins.then_inc(as_pw, 1)

            for m in range(4):
                dve.wait_ge(pair_free, U_GLU + m + 1)
                V.tensor_tensor(uT[:, m, :], zT[:, m, :], sgl[:, m % 2, :], ALU.mult).then_inc(os5_ready, 1)
            for m in range(KD):
                dve.wait_ge(pair_free, U_MIX + 4 * m + 4)
                A, B, N_, S_ = (mxb[:, m % 2, w, :] for w in range(4))
                V.tensor_tensor(A, A, N_, ALU.mult)
                link(V.tensor_tensor(B, B, S_, ALU.mult))
                V.tensor_tensor(mT[:, m, :], A, B, ALU.add).then_inc(mix_ready, 1)

            def post_norm(which, base, roots):
                dve.wait_ge(gain_in, 16 * (which + 1))
                for i, (kind, m) in enumerate(OUT_ORDER):
                    if kind == "t":
                        dve.wait_ge(pair_full, base + i + 1)
                        pr, c = pair(base + i), slice(P * m, P * m + P)
                        V.tensor_tensor(ytm[0:NB, TT, c], pr[0:NB, 1, 0:P], gain[0:NB, c], ALU.mult)
                        V.tensor_tensor(ytm[:, 0:TT, c], pr[:, 0, :].rearrange("p (t c) -> p t c", t=TT),
                                        gain[:, c].unsqueeze(1).to_broadcast([P, TT, P]),
                                        ALU.mult).then_inc(yg_ready, 1)
                dve.wait_ge(pair_free, base + len(OUT_ORDER))
                V.tensor_reduce(ssq[:, 0:TT], sqm[:, 0:TT, :], AX, ALU.add)
                V.tensor_reduce(ssq[0:NB, TT:5], sqm[0:NB, TT:5, :], AX, ALU.add).then_inc(ssq_ready, 1)
                dve.wait_ge(root_ready, roots + 1)
                V.reciprocal(rstd[:, 0:TT], ssq[:, 0:TT])
                link(V.reciprocal(rstd[0:NB, TT:5], ssq[0:NB, TT:5]))

                def add(t):
                    r = ROWS[t]
                    V.scalar_tensor_tensor(x1[0:r, t, :], ytm[0:r, t, :], rstd[0:r, t:t + 1], x1[0:r, t, :],
                                           ALU.mult, ALU.add).then_inc(x1_ready, 1)
                return add

            add = post_norm(0, U_OUT, 5)
            dve.wait_ge(x2_in, 32)
            pre_norm(10, x1, xn2, gT[:, 1, :], 6, add)
            for m in range(KF):
                dve.wait_ge(pair_free, U_UP + m + 1)
                V.tensor_tensor(fT[:, m, :], fT[:, m, :], fT[:, m, :], ALU.mult).then_inc(f_ready, 1)
            add = post_norm(1, U_DOWN, 11)
            for t in range(5):
                add(t)

        @block.tensor
        def _(pe):
            M = nc.tensor.matmul

            def tp(out, in_, rows=P):
                return nc.tensor.transpose(out, in_, ident[0:rows, 0:rows])

            def norm_transposes(first, src):
                for v0, (t, half) in enumerate(NORM_UNITS):
                    v = first + v0
                    r = ROWS[t]
                    pe.wait_ge(xn_ready, first // 2 + t + 1)
                    if v >= 4:
                        pe.wait_ge(xnt_free, v - 3)
                    for k in range(4):
                        ins = tp(PS[:, 4 + v % 4, r * k:r * k + r],
                                 src[0:r, t % 2, P * (4 * half + k):P * (4 * half + k) + P], r)
                    ins.then_inc(xnt_full, 1)

            def open_pair(u):
                if u >= 2:
                    pe.wait_ge(pair_free, u - 1)

            def gemm(u, lhs, rhs, w=P):
                n = len(lhs)
                for hf in range(2):
                    for k in range(n):
                        ins = M(pair(u)[0:w, hf, 0:HALF], lhs[k], rhs[k][:, HALF * hf:HALF * hf + HALF],
                                start=(k == 0), stop=(k == n - 1))
                return ins

            def back(u, src, w=P):
                for t in range(TT):
                    tp(pair(u)[:, 0, w * t:w * t + w], src[0:w, P * t:P * t + P], w)
                return tp(pair(u)[0:NB, 1, 0:w], src[0:w, T:NT], w)

            pe.wait_ge(consts_in, 16)
            norm_transposes(0, xn)
            pe.wait_ge(xnt_free, 10)

            last_of = {}
            for u, unit in enumerate(HEAD_UNITS + REST_UNITS):
                if unit[0] == "gemm":
                    last_of[SLAB[unit[1]]] = u

            def projection(u, unit):
                open_pair(u)
                kind = unit[0]
                pr = pair(u)
                if kind == "gemm":
                    _, key, m, w, to = unit
                    n = SLAB[key]
                    wait_slab(pe, n)
                    width = 512 if w == P else w
                    S = slab(n)[:, 0:KD * width].rearrange("p (k c) -> p k c", c=width)
                    ins = gemm(u, [S[:, k, P * m:P * m + w] for k in range(KD)], [hT[:, k, :] for k in range(KD)], w)
                    ins.then_inc(pair_full, 1)
                    if last_of[n] == u:
                        pe.wait_ge(pair_full, u + 1)
                        pe.sem_inc(slab_used, 1)
                    return
                if kind == "tr":
                    c, m = unit[1:]
                    src = kT[:, 2 * (c - 1) + m, :] if c > 0 and m < 2 else zst[:, m % 2, :]
                    ins = back(u, src)
                elif kind == "trg":
                    for t in range(TT):
                        tp(pr[:, 0, 48 * t:48 * t + 48], gsT[:, P * t:P * t + P], 48)
                    ins = tp(pr[0:NB, 1, 0:48], gsTs[0:48, :], 48)
                elif kind == "bb":
                    _, ri, q = unit
                    pe.wait_ge(bb_ready, 1)
                    for i in range(4):
                        ins = tp(pr[:, 0, P * i:P * i + P], BBP[:, ri, 4 * q + i, :])
                elif kind == "cc":
                    _, ri, q = unit
                    pe.wait_ge(c_in, 16 * 16)
                    for i in range(4):
                        ins = tp(pr[:, 0, P * i:P * i + P], CCP[:, ri, 4 * q + i, :])
                elif kind == "h0":
                    pe.wait_ge(h0_in, 16)
                    for i in range(NST):
                        for r in range(2):
                            ins = tp(pr[:, 0, 16 * i + 8 * r:16 * i + 8 * r + 8], st0[:, i, r, :], NB)
                else:
                    pe.wait_ge(pair_free, u - 1)
                    for i in range(NST):
                        for r in range(2):
                            ins = M(pr[:, 0, 16 * i + 8 * r:16 * i + 8 * r + 8], BBT[:, r, i, :],
                                    uT[:, i // 4, T:NT], start=True, stop=True)
                ins.then_inc(pair_full, 1)

            def s5_slot(i):
                if i < NST:
                    if i >= 1:
                        pe.wait_ge(bu_free, i)
                    M(PS[:, 4, :], BBT[:, 0, i, :], uT[:, i // 4, 0:T], start=True, stop=True)
                    M(PS[:, 5, :], BBT[:, 1, i, :], uT[:, i // 4, 0:T], start=True, stop=True).then_inc(bu_full, 1)
                if i >= 1:
                    i -= 1
                    q, ii = i // 4, i % 4
                    pe.wait_ge(h_ready, i + 1)
                    if ii == 0 and q:
                        pe.wait_ge(y_free, q)
                    for r in range(2):
                        h = W5[4 + 2 * (i % 2) + r]
                        s, e = ii == 0 and r == 0, ii == 3 and r == 1
                        M(PS[:, 6, :], CCT[:, r, i, :], h[:, 0:T], start=s, stop=e)
                        ins = M(PS[:, 7, 0:NB], CCT[:, r, i, :], h[:, T:NT], start=s, stop=e)
                    ins.then_inc(h_used, 1)
                    if e:
                        pe.wait_ge(h_used, i + 1)
                        pe.sem_inc(y_full, 1)

            for u, unit in enumerate(HEAD_UNITS):
                projection(u, unit)
            pe.wait_ge(pair_free, len(HEAD_UNITS))
            slot = 0
            for i, unit in enumerate(REST_UNITS):
                projection(len(HEAD_UNITS) + i, unit)
                if i % 2 == 1 and slot <= NST:
                    s5_slot(slot)
                    slot += 1
            while slot <= NST:
                s5_slot(slot)
                slot += 1
            pe.wait_ge(pair_free, UA)
            for v in range(8):
                if v >= 2:
                    pe.wait_ge(st_ready, v - 1)
                for i in range(2):
                    for r in range(2):
                        c0 = P * (2 * i + r)
                        ins = tp(PS[0:9, v % 2, c0:c0 + P], hS[:, 2 * v + i, r, :])
                ins.then_inc(st_full, 1)

            pe.wait_ge(w1_in, 16 * 14)
            pe.wait_ge(y_free, 4)
            for k in range(2):
                for s in range(16):
                    f = s // 8
                    ins = M(PS[0:64, 7, k:k + 1], w1c[:, k, s % 8, 64 * (f ^ k):64 * (f ^ k) + 64], peT[:, k, s:s + 1],
                            start=(s == 0), stop=(s == 15))
            ins.then_inc(pos_full, 1)

            def xpose(r):
                b, half, kind, s4 = RS[r]
                n = NCH if b < NB else NCP + 1
                w = r // 4
                if s4 == 0:
                    pe.wait_ge(perm_ready, w + 1)
                    if kind == 1:
                        pe.sem_inc(slab_used, 1)
                if r >= 3:
                    pe.wait_ge(xt_ready, r - 2)
                for g in range(4):
                    ins = tp(PS[:, 4 + r % 3, n * g:n * g + n],
                             ROWSP[0:n, w % 3, g, 2 * s4:2 * s4 + 2, :].rearrange("p s d -> p (s d)"), n)
                ins.then_inc(xt_full, 1)

            def layer1(r):
                b, half, kind, s4 = RS[r]
                n = 4 * (NCH if b < NB else NCP + 1)
                pe.wait_ge(xt_ready, r + 1)
                if b >= 2 and r % 16 == 0:
                    pe.wait_ge(l2_ready, b - 1)
                ins = M(PS[:, 2 * (b % 2) + kind, 0:n], w1c[:, kind, 4 * half + s4, :], XT[:, r % 3, 0:n],
                        start=(half == 0 and s4 == 0), stop=(half == 1 and s4 == 3))
                ins.then_inc(xt_used, 1)
                if r % 16 == 15:
                    pe.wait_ge(xt_used, r + 1)
                    pe.sem_inc(acc_full, 1)

            def layer2(b):
                n = NC if b < NB else NCP
                pe.wait_ge(gelu_ready, b + 1)
                M(PS[0:64, 2 * (b % 2), 0:4 * n], w2[0:64, :], GEL[0:64, 0:4 * n], start=True, stop=True)
                for g in range(4):
                    ins = M(PS[0:n, 2 * (b % 2) + 1, 64 * g:64 * g + 64], GEL[64:128, n * g:n * g + n], w2[64:128, :],
                            start=True, stop=True)
                ins.then_inc(l2_full, 1)

            pe.wait_ge(pos_full, 1)
            for r in range(N_RS + 1):
                if r < N_RS:
                    xpose(r)
                if r >= 1:
                    layer1(r - 1)
                if r >= 16 and r % 16 == 6:
                    layer2(r // 16 - 1)
            layer2(NB)

            pe.wait_ge(qpad_ready, 1)
            pe.wait_ge(l2_ready, NB + 1)
            BP = [(b, p) for b in range(NB) for p in range(2)]
            for i, (b, p) in enumerate(BP):
                M(PS[:, 5, 0:NC + 2], QP[:, p, b, :], kcT[:, b, p, :], start=(i == 0), stop=(i == 15))
            M(PS[:, 4, 0:3 * NH], consts[0:NB, CO_BMT:CO_BMT + P], gs8[0:NB, :], start=True,
              stop=True).then_inc(sc_full, 1)

            def key_t(r):
                q, b, p = KR[r]
                n = SLAB[("kpage", (q, b // 4)) if q < 4 else ("winrows", (0, b // 4))]
                if p == 0 and b % 4 == 0:
                    wait_slab(pe, n)
                S = slab(n).rearrange("p (b g c) -> p b g c", b=4, g=4)
                pe.wait_ge(xt_ready, N_RS + max(0, r - 1))
                for g in range(4):
                    ins = tp(PS[:, 6 + r % 2, P * g:P * g + P], S[:, b % 4, g, P * p:P * p + P])
                ins.then_inc(xt_full, 1)
                if p == 1 and b % 4 == 3:
                    pe.wait_ge(xt_full, N_RS + r + 1)
                    pe.sem_inc(slab_used, 1)

            def key_s(r):
                q, b, p = KR[r]
                pe.wait_ge(xt_ready, N_RS + r + 1)
                if r == 64:
                    pe.wait_ge(sc_max, 1)
                ins = M(PS[:, q, :], QP[:, p, b, :], XT[:, (N_RS + r) % 3, :],
                        start=(b == 0 and p == 0), stop=(b == NB - 1 and p == 1))
                ins.then_inc(xt_used, 1)
                if r % 16 == 15:
                    pe.wait_ge(xt_used, N_RS + r + 1)
                    pe.sem_inc(s_full, 1)

            for r in range(len(KR) + 1):
                if r < len(KR):
                    key_t(r)
                if r >= 1:
                    key_s(r - 1)
                if r == R_IMP:
                    pe.wait_ge(pc_ready, 1)
                    M(PS[0:32, 5, 0:NC], consts[:, CO_HSUM:CO_HSUM + 32], SC[:, 0:NC], start=True,
                      stop=True).then_inc(imp_full, 1)
                if r in R_CS:
                    t = R_CS.index(r)
                    if t == 0:
                        pe.wait_ge(selx_read, 1)
                    else:
                        pe.wait_ge(cs_max, t)
                    for p in range(2):
                        for h in range(HPG):
                            c = 2 * NCP * (HPG * p + h)
                            ins = M(PS[:, 5, c:c + 2 * NCP], qT[:, 4 * p + h, P * t:P * t + P],
                                    KCZ[:, p].rearrange("p j n -> p (j n)"), start=True, stop=True)
                    ins.then_inc(cs_full, 1)
                if r == R_SEL:
                    pe.wait_ge(sel_ready, 1)
                    M(PS[:, 5, 0:NSEL], consts[0:32, CO_HSUMT:CO_HSUMT + P], SSEL, start=True,
                      stop=True).then_inc(selx_full, 1)
            pe.wait_ge(pa_ready, 1)
            for v in range(6):
                if v == 4:
                    pe.wait_ge(p_ready, 1)
                bank = PT_BANK[v]
                for g in range(4 if v < 5 else 0):
                    src = SA[:, P * (4 * v + g):P * (4 * v + g) + P] if v < 4 else SW[:, P * g:P * g + P]
                    ins = tp(PS[:, bank, P * g:P * g + P], src)
                if v == 5:
                    tp(PS[0:NC, bank, 0:P], SC[:, 0:NC])
                    tp(PS[0:NB, bank, P:2 * P], PNB[:, 0])
                    ins = tp(PS[0:NB, bank, 2 * P:3 * P], PNB[:, 1])
                ins.then_inc(pt_full, 1)
            pe.wait_ge(pt_ready, 6)
            def out_bank(r, b):
                return PS[0:NH, 4 * r + b // 2, 256 * (b % 2):256 * (b % 2) + 256]

            def new_token(r, b):
                c0 = KVW * (1 + r) + 256
                M(out_bank(r, b), PTN[:, r, NH * b:NH * b + NH], kvs[:, c0:c0 + 256], start=True, stop=False)

            for b in range(NB):
                n = SLAB[("winrows", (1, b // 4))]
                if b % 4 == 0:
                    wait_slab(pe, n)
                S = slab(n).rearrange("p (b g c) -> p b g c", b=4, g=4)
                new_token(1, b)
                for g in range(4):
                    ins = M(out_bank(1, b), PTA[:, 16 + g, NH * b:NH * b + NH], S[:, b % 4, g, :],
                            start=False, stop=(g == 3))
                if b % 4 == 3:
                    ins.then_inc(slab_used, 1)
            pe.wait_ge(slab_used, SLAB[("winrows", (1, 1))] + 1)
            pe.sem_inc(oe_full, 1)
            for b in range(NB):
                n = SLAB[("vpage", (b,))]
                new_token(0, b)
                M(out_bank(0, b), PTC[0:NC, NH * b:NH * b + NH], vc[0:NC, b, :], start=False, stop=False)
                wait_slab(pe, n)
                S = slab(n).rearrange("p (x c) -> p x c", x=16)
                for x in range(16):
                    ins = M(out_bank(0, b), PTA[:, x, NH * b:NH * b + NH], S[:, x, :], start=False, stop=(x == 15))
                ins.then_inc(slab_used, 1)
            pe.wait_ge(slab_used, SLAB[("vpage", (NB - 1,))] + 1)
            pe.sem_inc(od_full, 1)

            pe.wait_ge(od_ready, 1)
            pe.wait_ge(kz_ready, 2)

            def scores(n):
                t, p, h, j, nx = TASKS[n]
                if n >= 2:
                    pe.wait_ge(as_exp, n - 1)
                for i, x, r, bank, c0 in softmaxes(n):
                    S = PS[:, 1 + 2 * (n % 2) + bank, c0:c0 + P * (t + 1)]
                    M(S, qT[:, 4 * p + h + x, P * t:P * t + P], KZ[:, j, 2 * r + p, 0:P * (t + 1)],
                      start=True, stop=False)
                    ins = M(S[:, P * t:P * t + P], idb[:, :], maskb[:, :], start=False, stop=True)
                ins.then_inc(as_full, 1)

            def probs(n):
                t, p, h, j, nx = TASKS[n]
                if n >= 1:
                    pe.wait_ge(at_a, n)
                    pe.wait_ge(at_d, n)
                for x in range(nx):
                    tp(PS[0:NCP, 0, P * x:P * x + P], PCP[:, t, (2 * p + j) * HPG + h + x, :])
                for r in range(2):
                    pe.wait_ge(as_pw if r else as_p, n + 1)
                    for i, x, r_, bank, c0 in softmaxes(n):
                        if r_ == r:
                            for k in range(t + 1):
                                c = c0 + P * k
                                ins = tp(PS[:, 5 + bank, c:c + P], PP[:, n % 2, bank, c:c + P])
                ins.then_inc(at_full, 1)

            def values(n):
                t, p, h, j, nx = TASKS[n]
                g = 2 * p + j
                pe.wait_ge(at_a, n + 1)
                pe.wait_ge(at_d, n + 1)
                if n >= 1:
                    pe.wait_ge(ao_free, n)
                for x in range(nx):
                    first = True
                    out = PS[0:64, 7, P * x:P * x + P]
                    for i, x_, r, bank, c0 in softmaxes(n):
                        if x_ != x:
                            continue
                        for k in range(t + 1):
                            v0, c = 256 * r + 64 * g, c0 + P * k
                            M(out, vtm[:, k, v0:v0 + 64], PTP[:, n % 2, bank, c:c + P], start=first, stop=False)
                            first = False
                    ins = M(out, vc[0:NCP, NB, 64 * g:64 * g + 64], PTPC[0:NCP, n % 2, P * x:P * x + P],
                            start=False, stop=True)
                ins.then_inc(ao_full, 1)

            for n in range(NTK + 2):
                if n < NTK:
                    scores(n)
                if n == 0:
                    pe.wait_ge(ot_ready, 1)
                    for b in range(NB):
                        ins = tp(PS[0:DH, 7, NH * b:NH * b + NH], OS[:, b, :], NH)
                    ins.then_inc(ot_full, 1)
                if n == 2:
                    pe.wait_ge(ot_done, 1)
                if 1 <= n <= NTK:
                    probs(n - 1)
                if n >= 2:
                    values(n - 2)
            pe.wait_ge(ao_free, NTK)

            n = SLAB[("glu", ())]
            wait_slab(pe, n)
            pe.wait_ge(z_ready, 1)
            S = slab(n)[:, 0:2048].rearrange("p (k c) -> p k c", k=4)
            for m in range(4):
                open_pair(U_GLU + m)
                ins = gemm(U_GLU + m, [S[:, k, P * m:P * m + P] for k in range(4)], [zT[:, k, :] for k in range(4)])
                ins.then_inc(pair_full, 1)
            pe.wait_ge(pair_full, U_GLU + 4)
            pe.sem_inc(slab_used, 1)
            for m in range(KD):
                n = SLAB[("mix", (m,))]
                wait_slab(pe, n)
                S = slab(n)[:, 0:3 * D].rearrange("p (w k c) -> p w k c", w=3, c=P)
                S5 = slab(n)[:, 3 * D:3 * D + 512].rearrange("p (k c) -> p k c", c=P)
                for w in range(4):
                    u = U_MIX + 4 * m + w
                    open_pair(u)
                    if m == 0 and w == 3:
                        pe.wait_ge(os5_ready, 4)
                    src = (hT, hT, oT, uT)[w]
                    nk = KD if w < 3 else 4
                    ins = gemm(u, [(S[:, w, k, :] if w < 3 else S5[:, k, :]) for k in range(nk)],
                               [src[:, k, :] for k in range(nk)])
                    ins.then_inc(pair_full, 1)
                pe.wait_ge(pair_full, U_MIX + 4 * m + 4)
                pe.sem_inc(slab_used, 1)

            def out_units(base, key, kt, per, src, stage):
                for i, (kind, m) in enumerate(OUT_ORDER):
                    u = base + i
                    open_pair(u)
                    if kind == "g":
                        n = SLAB[(key, (m // per,))]
                        wait_slab(pe, n)
                        S = slab(n).rearrange("p (k c) -> p k c", k=kt)
                        c = P * (m % per)
                        ins = gemm(u, [S[:, k, c:c + P] for k in range(kt)], [src[:, k, :] for k in range(kt)])
                        ins.then_inc(pair_full, 1)
                        if m % per == per - 1:
                            pe.wait_ge(pair_full, u + 1)
                            pe.sem_inc(slab_used, 1)
                    else:
                        back(u, stage[:, m % 2, :]).then_inc(pair_full, 1)

            pe.wait_ge(mix_ready, KD)
            out_units(U_OUT, "out", KD, 4, mT, zo)
            norm_transposes(10, xn2)
            pe.wait_ge(xnt_free, 20)
            for m in range(KF):
                u = U_UP + m
                open_pair(u)
                n = SLAB[("up", (m // 4,))]
                wait_slab(pe, n)
                S = slab(n).rearrange("p (k c) -> p k c", k=KD)
                c = P * (m % 4)
                ins = gemm(u, [S[:, k, c:c + P] for k in range(KD)], [hT[:, k, :] for k in range(KD)])
                ins.then_inc(pair_full, 1)
                if m % 4 == 3:
                    pe.wait_ge(pair_full, u + 1)
                    pe.sem_inc(slab_used, 1)
            pe.wait_ge(f_ready, KF)
            out_units(U_DOWN, "down", KF, 1, fT, hT)


INPUTS = ["x_prompt", "x_sample", "cache_kv_cmp", "cache_kv_slc", "state_kv_win", "state_s5", "page_table",
          "norm_mix_pre", "norm_mix_post", "norm_mlp_pre", "norm_mlp_post", "w_in",
          "cmp_pe_k", "cmp_w1_k", "cmp_w2_k", "cmp_pe_v", "cmp_w1_v", "cmp_w2_v",
          "s5_a_re", "s5_a_im", "s5_log_dt", "s5_b_re", "s5_b_im", "s5_c_re", "s5_c_im", "s5_d", "s5_w_glu",
          "s5_b_glu", "w_branch_nsa", "w_branch_s5", "w_out", "w_mlp_up", "w_mlp_down"]
KVS = (2, NG, DH)
OUTPUTS = [("y_prompt", (1, T, D)), ("y_sample", (NB, 1, D)),
           ("kv_cmp_prompt", (1, T) + KVS), ("kv_slc_prompt", (1, T) + KVS), ("kv_win_prompt", (1, WIN) + KVS),
           ("s5_prompt", (1, G5, N5, 2)),
           ("kv_cmp_sample", (NB, 1) + KVS), ("kv_slc_sample", (NB, 1) + KVS), ("kv_win_sample", (NB, WIN) + KVS),
           ("s5_sample", (NB, G5, N5, 2))]


def kernel(**inputs):
    import concourse.bacc as bacc
    from concourse.bass_utils import run_bass_kernel_spmd

    nc = bacc.Bacc("TRN2", target_bir_lowering=False, num_devices=1)
    consts, tie = shape_constants()
    arrays, aps = {}, {}
    given = {name: np.ascontiguousarray(inputs[name]) for name in INPUTS}
    given["consts"], given["tie"] = consts, tie
    for name, v in given.items():
        arrays[f"in_{name}"] = v
        aps[name] = nc.dram_tensor(f"in_{name}", v.shape, mybir.dt.from_np(v.dtype), kind="ExternalInput").ap()
    for name, shape in OUTPUTS:
        aps[name] = nc.dram_tensor(f"out_{name}", shape, F32, kind="ExternalOutput").ap()
    build(nc, aps)
    r = run_bass_kernel_spmd(nc, [arrays], core_ids=[0])
    return tuple(r.results[0][f"out_{name}"] for name, _ in OUTPUTS)
```
